# Optimizing a Trainium2 kernel written in Bass

```python
import jax, jax.numpy as jnp
from jax import lax
import numpy as np

D_MODEL = 1024
BATCH = 1
SEQ = 1024
DEPTH = 1
DEC_BATCH = 8
DEC_SEQ = 8
PAST_LEN = 2048
PAGE_SIZE = 128

N_HEADS_A = 8
HEAD_DIM_A = 64
WIDTH_A = N_HEADS_A * HEAD_DIM_A
Q_BLOCK = 128
FORGET_BIAS = 7.0
N_GROUPS_B = 8
WIDTH_B = 512
GROUP_DIM_B = WIDTH_B // N_GROUPS_B
CHUNK = 128
N_EXPERT_GROUPS = 4
EXPERTS_PER_GROUP = 8
N_EXPERTS = N_EXPERT_GROUPS * EXPERTS_PER_GROUP
TOP_K = 2
D_FF_EXPERT = 512
DISPATCH_BLOCK = 128
PLE_DIM = 256
EPS = 1e-6
OFF_Q = 0
OFF_K = OFF_Q + WIDTH_A
OFF_V = OFF_K + WIDTH_A
OFF_F = OFF_V + WIDTH_A
OFF_U = OFF_F + N_HEADS_A
OFF_VB = OFF_U + WIDTH_B
OFF_GA = OFF_VB + WIDTH_B
OFF_GB = OFF_GA + D_MODEL
PROJ_COLS = OFF_GB + D_MODEL

kernel_name = 'fox_gmlp_hiermoe_hybrid_step'

def rmsnorm(x, g):
    xf = x.astype(jnp.float32)
    y = xf * lax.rsqrt(jnp.mean(xf * xf, axis=-1, keepdims=True) + EPS)
    return (y * g.astype(jnp.float32)).astype(x.dtype)

def layernorm(x, g, b):
    xf = x.astype(jnp.float32)
    mu = jnp.mean(xf, axis=-1, keepdims=True)
    xc = xf - mu
    y = xc * lax.rsqrt(jnp.mean(xc * xc, axis=-1, keepdims=True) + EPS)
    return (y * g.astype(jnp.float32) + b.astype(jnp.float32)).astype(x.dtype)

def project_inputs(h, w_in, b_f):
    B, S = h.shape[0], h.shape[1]
    proj = jnp.einsum('bsd,dc->bsc', h, w_in)
    q = proj[..., OFF_Q:OFF_K].reshape(B, S, N_HEADS_A, HEAD_DIM_A)
    k = proj[..., OFF_K:OFF_V].reshape(B, S, N_HEADS_A, HEAD_DIM_A)
    v = proj[..., OFF_V:OFF_F].reshape(B, S, N_HEADS_A, HEAD_DIM_A)
    logf = jax.nn.log_sigmoid((proj[..., OFF_F:OFF_U] + b_f).astype(jnp.float32))
    u = proj[..., OFF_U:OFF_VB]
    vb = proj[..., OFF_VB:OFF_GA]
    ga = jax.nn.sigmoid(proj[..., OFF_GA:OFF_GB])
    gb = jax.nn.sigmoid(proj[..., OFF_GB:PROJ_COLS])
    return q, k, v, logf, u, vb, ga, gb

def fox_prompt(q, k, v, logf):
    B, S, H, Dh = q.shape
    nb = S // Q_BLOCK
    scale = Dh ** -0.5
    c = jnp.cumsum(logf, axis=1).transpose(0, 2, 1)
    key_pos = jnp.arange(S)
    qb = q.reshape(B, nb, Q_BLOCK, H, Dh).transpose(1, 0, 2, 3, 4)
    cb = c.reshape(B, H, nb, Q_BLOCK).transpose(2, 0, 1, 3)
    pb = key_pos.reshape(nb, Q_BLOCK)

    def block(args):
        qi, ci, pi = args
        s = jnp.einsum('bqhd,bkhd->bhqk', qi, k).astype(jnp.float32) * scale
        s = s + ci[..., :, None] - c[:, :, None, :]
        s = jnp.where(pi[:, None] >= key_pos[None, :], s, -jnp.inf)
        p = jax.nn.softmax(s, axis=-1)
        return jnp.einsum('bhqk,bkhd->bqhd', p.astype(v.dtype), v)

    o = lax.map(block, (qb, cb, pb))
    return o.transpose(1, 0, 2, 3, 4).reshape(B, S, H * Dh)

def fox_sample(q, k, v, logf, cache_k, cache_v, cache_logf, page_table):
    DB, T, H, Dh = q.shape
    past = page_table.shape[1] * cache_k.shape[1]
    scale = Dh ** -0.5
    kp = cache_k[page_table].reshape(DB, past, H, Dh)
    vp = cache_v[page_table].reshape(DB, past, H, Dh)
    lfp = cache_logf[page_table].reshape(DB, past, H).astype(jnp.float32)
    suffix = (lax.cumsum(lfp, axis=1, reverse=True) - lfp).transpose(0, 2, 1)
    cn = jnp.cumsum(logf, axis=1).transpose(0, 2, 1)
    s_past = jnp.einsum('bqhd,bkhd->bhqk', q, kp).astype(jnp.float32) * scale
    s_past = s_past + suffix[:, :, None, :] + cn[:, :, :, None]
    s_new = jnp.einsum('bqhd,bkhd->bhqk', q, k).astype(jnp.float32) * scale
    s_new = s_new + cn[:, :, :, None] - cn[:, :, None, :]
    causal = jnp.tril(jnp.ones((T, T), dtype=bool))
    s_new = jnp.where(causal, s_new, -jnp.inf)
    p = jax.nn.softmax(jnp.concatenate([s_past, s_new], axis=-1), axis=-1)
    o = (jnp.einsum('bhqk,bkhd->bqhd', p[..., :past].astype(v.dtype), vp)
         + jnp.einsum('bhqk,bkhd->bqhd', p[..., past:].astype(v.dtype), v))
    return o.reshape(DB, T, H * Dh)

def chunk_mlp(u, vb, ln_g, ln_b, w_s, b_s):
    B, S, _ = u.shape
    L = min(S, CHUNK)
    nc = S // L
    ug = jax.nn.gelu(u)
    v = layernorm(jax.nn.gelu(vb), ln_g, ln_b)
    vc = v.reshape(B, nc, L, N_GROUPS_B, GROUP_DIM_B)
    w = w_s[:, :L, :L] * jnp.tril(jnp.ones((L, L), dtype=w_s.dtype))
    sv = jnp.einsum('gts,bcsgd->bctgd', w, vc) + b_s[:, :L].T[:, :, None]
    return ug * sv.reshape(B, S, WIDTH_B), v

def merge_branches(x, a_out, b_out, ga, gb, w_up_a, w_up_b, w_o):
    m = ga * (a_out @ w_up_a) + gb * (b_out @ w_up_b)
    return x + m @ w_o

def hier_moe(h, w_rg, b_rg, w_re, b_re, w_g, w_u, w_d):
    T, D = h.shape
    hf = h.astype(jnp.float32)
    glog = hf @ w_rg.astype(jnp.float32) + b_rg.astype(jnp.float32)
    gprob = jax.nn.softmax(glog, axis=-1)
    gsel = jnp.argmax(glog, axis=-1).astype(jnp.int32)
    pg = jnp.take_along_axis(gprob, gsel[:, None], axis=1)[:, 0]
    elog = (hf @ w_re.astype(jnp.float32) + b_re.astype(jnp.float32)).reshape(T, N_EXPERT_GROUPS, EXPERTS_PER_GROUP)
    elog = jnp.take_along_axis(elog, gsel[:, None, None], axis=1)[:, 0]
    eprob = jax.nn.softmax(elog, axis=-1)
    topv, topi = lax.top_k(eprob, TOP_K)
    topv = topv / jnp.sum(topv, axis=-1, keepdims=True)
    expert_idx = gsel[:, None] * EXPERTS_PER_GROUP + topi.astype(jnp.int32)
    wts = pg[:, None] * topv

    N = T * TOP_K
    flat_e = expert_idx.reshape(N)
    flat_tok = jnp.arange(N, dtype=jnp.int32) // TOP_K
    flat_w = wts.reshape(N)
    order = jnp.argsort(flat_e)
    se = flat_e[order]
    counts = jnp.zeros((N_EXPERTS,), jnp.int32).at[flat_e].add(1)
    padded = (counts + DISPATCH_BLOCK - 1) // DISPATCH_BLOCK * DISPATCH_BLOCK
    start = jnp.cumsum(counts) - counts
    pend = jnp.cumsum(padded)
    pstart = pend - padded
    dest = pstart[se] + (jnp.arange(N, dtype=jnp.int32) - start[se])
    nb = -(-(N + N_EXPERTS * (DISPATCH_BLOCK - 1)) // DISPATCH_BLOCK)
    P = nb * DISPATCH_BLOCK
    slot_tok = jnp.full((P,), T, jnp.int32).at[dest].set(flat_tok[order])
    slot_w = jnp.zeros((P,), jnp.float32).at[dest].set(flat_w[order])
    block_start = jnp.arange(nb, dtype=jnp.int32) * DISPATCH_BLOCK
    block_e = jnp.minimum(jnp.searchsorted(pend, block_start, side='right'), N_EXPERTS - 1)
    hp = jnp.concatenate([h, jnp.zeros((1, D), h.dtype)], axis=0)
    xb = hp[slot_tok].reshape(nb, DISPATCH_BLOCK, D)

    def run_block(args):
        xi, e = args
        return (jax.nn.silu(xi @ w_g[e]) * (xi @ w_u[e])) @ w_d[e]

    yb = lax.map(run_block, (xb, block_e)).reshape(P, D)
    out = jnp.zeros((T + 1, D), jnp.float32).at[slot_tok].add(yb.astype(jnp.float32) * slot_w[:, None])
    return out[:T].astype(h.dtype)

def channel_and_ple(x, p_i, norm_moe_g, w_rg, b_rg, w_re, b_re, w_g, w_u, w_d,
                    norm_ple_g, w_ple_gate, b_ple_gate, w_ple_proj, norm_ple_post_g):
    B, S, D = x.shape
    h = rmsnorm(x, norm_moe_g).reshape(B * S, D)
    x = x + hier_moe(h, w_rg, b_rg, w_re, b_re, w_g, w_u, w_d).reshape(B, S, D)
    gate = jax.nn.sigmoid(rmsnorm(x, norm_ple_g) @ w_ple_gate + b_ple_gate)
    e = rmsnorm(p_i @ w_ple_proj, norm_ple_post_g)
    return x + gate * e

def setup_inputs(seed: int = 0) -> dict:
    key = jax.random.key(seed)
    ks = jax.random.split(key, 40)
    n_pages = PAST_LEN // PAGE_SIZE
    n_used = DEC_BATCH * n_pages
    n_pool = (n_used * 5) // 4

    def nrm(k, shape, scale=1.0):
        return jax.random.normal(k, shape, jnp.float32) * scale

    page_table = jax.random.permutation(ks[8], n_pool)[:n_used].reshape(DEC_BATCH, n_pages).astype(jnp.int32)
    return {
        'x_prompt': nrm(ks[0], (BATCH, SEQ, D_MODEL)),
        'x_sample': nrm(ks[1], (DEC_BATCH, DEC_SEQ, D_MODEL)),
        'p_prompt': nrm(ks[2], (DEPTH, BATCH, SEQ, PLE_DIM)),
        'p_sample': nrm(ks[3], (DEPTH, DEC_BATCH, DEC_SEQ, PLE_DIM)),
        'cache_k': nrm(ks[4], (DEPTH, n_pool, PAGE_SIZE, N_HEADS_A, HEAD_DIM_A)),
        'cache_v': nrm(ks[5], (DEPTH, n_pool, PAGE_SIZE, N_HEADS_A, HEAD_DIM_A)),
        'cache_logf': jax.nn.log_sigmoid(FORGET_BIAS + nrm(ks[6], (DEPTH, n_pool, PAGE_SIZE, N_HEADS_A), 0.5)),
        'page_table': page_table,
        'norm_mix_g': 1.0 + nrm(ks[9], (DEPTH, D_MODEL), 0.05),
        'w_in': nrm(ks[10], (DEPTH, D_MODEL, PROJ_COLS), D_MODEL ** -0.5),
        'b_f': FORGET_BIAS + nrm(ks[11], (DEPTH, N_HEADS_A), 0.5),
        'ln_v_g': 1.0 + nrm(ks[12], (DEPTH, WIDTH_B), 0.05),
        'ln_v_b': nrm(ks[13], (DEPTH, WIDTH_B), 0.02),
        'w_spatial': nrm(ks[14], (DEPTH, N_GROUPS_B, CHUNK, CHUNK), 0.5 * CHUNK ** -0.5),
        'b_spatial': 1.0 + nrm(ks[15], (DEPTH, N_GROUPS_B, CHUNK), 0.05),
        'w_up_a': nrm(ks[16], (DEPTH, WIDTH_A, D_MODEL), WIDTH_A ** -0.5),
        'w_up_b': nrm(ks[17], (DEPTH, WIDTH_B, D_MODEL), WIDTH_B ** -0.5),
        'w_o': nrm(ks[18], (DEPTH, D_MODEL, D_MODEL), D_MODEL ** -0.5),
        'norm_moe_g': 1.0 + nrm(ks[19], (DEPTH, D_MODEL), 0.05),
        'w_router_group': nrm(ks[20], (DEPTH, D_MODEL, N_EXPERT_GROUPS), D_MODEL ** -0.5),
        'b_router_group': nrm(ks[21], (DEPTH, N_EXPERT_GROUPS), 0.01),
        'w_router_expert': nrm(ks[22], (DEPTH, D_MODEL, N_EXPERTS), D_MODEL ** -0.5),
        'b_router_expert': nrm(ks[23], (DEPTH, N_EXPERTS), 0.01),
        'w_exp_gate': nrm(ks[24], (DEPTH, N_EXPERTS, D_MODEL, D_FF_EXPERT), D_MODEL ** -0.5),
        'w_exp_up': nrm(ks[25], (DEPTH, N_EXPERTS, D_MODEL, D_FF_EXPERT), D_MODEL ** -0.5),
        'w_exp_down': nrm(ks[26], (DEPTH, N_EXPERTS, D_FF_EXPERT, D_MODEL), D_FF_EXPERT ** -0.5),
        'norm_ple_g': 1.0 + nrm(ks[27], (DEPTH, D_MODEL), 0.05),
        'w_ple_gate': nrm(ks[28], (DEPTH, D_MODEL, D_MODEL), D_MODEL ** -0.5),
        'b_ple_gate': nrm(ks[29], (DEPTH, D_MODEL), 0.02),
        'w_ple_proj': nrm(ks[30], (DEPTH, PLE_DIM, D_MODEL), PLE_DIM ** -0.5),
        'norm_ple_post_g': 1.0 + nrm(ks[31], (DEPTH, D_MODEL), 0.05),
        'norm_final_g': 1.0 + nrm(ks[32], (D_MODEL,), 0.05),
    }

def reference(x_prompt, x_sample, p_prompt, p_sample, cache_k, cache_v, cache_logf, page_table,
              norm_mix_g, w_in, b_f, ln_v_g, ln_v_b, w_spatial, b_spatial, w_up_a, w_up_b, w_o,
              norm_moe_g, w_router_group, b_router_group, w_router_expert, b_router_expert,
              w_exp_gate, w_exp_up, w_exp_down, norm_ple_g, w_ple_gate, b_ple_gate, w_ple_proj,
              norm_ple_post_g, norm_final_g):
    xp = x_prompt
    xs = x_sample
    kp_l, vp_l, lfp_l, ks_l, vs_l, lfs_l, cvs_l = [], [], [], [], [], [], []
    for i in range(DEPTH):
        hp = rmsnorm(xp, norm_mix_g[i])
        q, k, v, lf, u, vb, ga, gb = project_inputs(hp, w_in[i], b_f[i])
        a_out = fox_prompt(q, k, v, lf)
        b_out, _ = chunk_mlp(u, vb, ln_v_g[i], ln_v_b[i], w_spatial[i], b_spatial[i])
        xp = merge_branches(xp, a_out, b_out, ga, gb, w_up_a[i], w_up_b[i], w_o[i])
        kp_l.append(k)
        vp_l.append(v)
        lfp_l.append(lf)
        hs = rmsnorm(xs, norm_mix_g[i])
        q, k, v, lf, u, vb, ga, gb = project_inputs(hs, w_in[i], b_f[i])
        a_out = fox_sample(q, k, v, lf, cache_k[i], cache_v[i], cache_logf[i], page_table)
        b_out, v_rows = chunk_mlp(u, vb, ln_v_g[i], ln_v_b[i], w_spatial[i], b_spatial[i])
        xs = merge_branches(xs, a_out, b_out, ga, gb, w_up_a[i], w_up_b[i], w_o[i])
        ks_l.append(k)
        vs_l.append(v)
        lfs_l.append(lf)
        cvs_l.append(v_rows)
        xp = channel_and_ple(xp, p_prompt[i], norm_moe_g[i], w_router_group[i], b_router_group[i],
                             w_router_expert[i], b_router_expert[i], w_exp_gate[i], w_exp_up[i],
                             w_exp_down[i], norm_ple_g[i], w_ple_gate[i], b_ple_gate[i],
                             w_ple_proj[i], norm_ple_post_g[i])
        xs = channel_and_ple(xs, p_sample[i], norm_moe_g[i], w_router_group[i], b_router_group[i],
                             w_router_expert[i], b_router_expert[i], w_exp_gate[i], w_exp_up[i],
                             w_exp_down[i], norm_ple_g[i], w_ple_gate[i], b_ple_gate[i],
                             w_ple_proj[i], norm_ple_post_g[i])
    y_prompt = rmsnorm(xp, norm_final_g)
    y_sample = rmsnorm(xs, norm_final_g)
    return (y_prompt, y_sample, jnp.stack(kp_l), jnp.stack(vp_l), jnp.stack(lfp_l),
            jnp.stack(ks_l), jnp.stack(vs_l), jnp.stack(lfs_l), jnp.stack(cvs_l))


_drawn_inputs = setup_inputs


def setup_inputs(seed=0):
    import zlib

    import numpy as np

    out = dict(_drawn_inputs(seed))
    spreads = {}
    factors = {'cache_k': 2.857,
     'cache_logf': 159.535,
     'ln_v_b': 2.874,
     'b_router_group': 14.876,
     'b_router_expert': 3.535,
     'norm_ple_g': 7.105,
     'b_ple_gate': 39.55}
    for name, (base, spread) in spreads.items():
        noise = np.random.default_rng([zlib.crc32(name.encode()), seed]).standard_normal(out[name].shape)
        drawn = base * np.exp(spread * noise) if base else spread * noise
        out[name] = __import__('jax').numpy.asarray(drawn.astype(out[name].dtype))
    for name, factor in factors.items():
        out[name] = (out[name] * factor).astype(out[name].dtype)
    return out
```

```python
from contextlib import ExitStack

import numpy as np
import concourse.bass as bass
from concourse import mybir

F32 = mybir.dt.float32
BF16 = mybir.dt.bfloat16
I32 = mybir.dt.int32
U32 = mybir.dt.uint32
ALU = mybir.AluOpType
ACT = mybir.ActivationFunctionType
AX = mybir.AxisListType

P = 128
D = 1024
KD = D // P
SEQ = 1024
DB, DT = 8, 8
NS = DB * DT
NP = SEQ // P
NT = NP + 1
TOK = NT * P
H, DH = 8, 64
WA = H * DH
NPAIR = H // 2
PAGES = 16
PAST = PAGES * P
NG, NEG = 4, 8
NE = NG * NEG
FF = 512
KF = FF // P
PLE = 256
EPS = 1e-6
SCALE = DH ** -0.5
BIG = 1e30
OFF_F = 3 * WA
OFF_U = OFF_F + H
OFF_VB = OFF_U + WA
OFF_GA = OFF_VB + WA
OFF_GB = OFF_GA + D
BLK = P
NOVER = (2 * (SEQ + NS) - 1) // BLK
SLOTS = (NE + NOVER) * P

HT_AT = 0
W_AT = HT_AT + TOK * KD
WBLK = KD * 512
Q_AT = W_AT + 4 * WBLK
K_AT = Q_AT + NT * WA
V_AT = K_AT + NT * WA
A_AT = V_AT + NT * WA
B_AT = A_AT + NT * WA
T_AT = B_AT + NT * WA
T_END = T_AT + 3300


class Core:
    pass


def bcast(ap, n):
    return ap.unsqueeze(2).to_broadcast([ap.shape[0], ap.shape[1], n])


def start(nc, c, ctx):
    def sb(name, shape, dt=F32):
        return ctx.enter_context(nc.sbuf_tensor(name, shape, dt))

    c.local = []

    def stage_semaphore(name):
        c.local.append(nc.alloc_semaphore(name=name))
        return c.local[-1]

    c.sem = stage_semaphore
    c.kept_sem = lambda name: ctx.enter_context(nc.semaphore(name))
    c.arena = sb("arena", [P, T_END])
    psum = ctx.enter_context(nc.psum_tensor("psum", [P, 8 * 512], F32))
    c.bank = [psum[:, i * 512:(i + 1) * 512] for i in range(8)]
    c.psum_pair = lambda i: psum[:, i * 1024:(i + 1) * 1024]
    c.ident = sb("ident", [P, P])
    c.ident_b = sb("ident_b", [P, P], BF16)
    c.future_b = sb("future_b", [P, P], BF16)
    c.before = sb("before", [P, P])
    c.ones = sb("ones", [P, P])
    c.g_mix = sb("g_mix", [P, KD])
    c.g_moe = sb("g_moe", [P, KD])
    c.g_ple = sb("g_ple", [P, KD])
    c.stat = sb("stat", [P, 4, NT])
    c.neghalf = sb("neghalf", [P, NT])
    c.new_mask = sb("new_mask", [NS, 2 * NS])
    c.w_route = sb("w_route", [P, KD, NG + NE])
    c.b_route = sb("b_route", [P, NG + NE])


def release(nc, c):
    nc.clear_and_free_semaphores(c.local)
    c.local.clear()
    nc.all_engine_barrier()


def view(c, at, *dims):
    n = int(np.prod(dims))
    v = c.arena[:, at:at + n]
    if len(dims) == 1:
        return v
    names = "abcd"[:len(dims)]
    return v.rearrange(f"p ({' '.join(names)}) -> p {' '.join(names)}",
                       **{k: d for k, d in zip(names, dims)})


def rows(x, at, n, width=None):
    return x[at:at + n, :]


def stage_norm(nc, c):
    X = view(c, Q_AT, NT, D)
    HT = view(c, HT_AT, NT, KD, P)
    W = view(c, W_AT, 4, KD, 512)
    LF = view(c, A_AT, P, H)
    PRE = view(c, A_AT + 1024, H, P)
    NB = view(c, A_AT + 2048, H, P)
    pidx = view(c, A_AT + 3072, 1).bitcast(I32)
    later = view(c, A_AT + 3080, P)
    carry = view(c, A_AT + 3208, H)
    junk = view(c, B_AT, D)
    x_in = [c.sem(f"x_in{t}") for t in range(NT)]
    pad_zero, gains_in, ss_done = c.sem("pad_zero"), c.sem("gains_in"), c.sem("ss_done")
    rstd_done, xn_done, tr_done, ht_done = (c.sem("rstd_done"), c.sem("xn_done"),
                                            c.sem("tr_done"), c.sem("ht_done"))
    ident_zero, ident_done, const_step = c.sem("ident_zero"), c.sem("ident_done"), c.sem("const_step")
    pidx_in, logf_in, scan_done = c.sem("pidx_in"), c.sem("logf_in"), c.sem("scan_done")
    carry_mm, carry_done, nb_done = c.sem("carry_mm"), c.sem("carry_done"), c.sem("nb_done")
    c.w_in_sem = [c.kept_sem(f"w_slot{i}") for i in range(4)]
    c.sufd_out = c.kept_sem("sufd_out")
    c.consts_in = c.kept_sem("consts_in")
    dve_step = c.sem("norm_dve_step")
    ms_done = c.sem("ms_done")
    with nc.Block() as block:
        @block.sync
        def _(sp):
            for t in range(NP):
                sp.dma_start(X[:, t, :], c.x_prompt[t * P:(t + 1) * P, :]).then_inc(x_in[t], 16)
            sp.dma_start(X[0:NS, NP, :], c.x_sample).then_inc(x_in[NP], 16)
            for s, col in enumerate((0, 2 * WA, WA, OFF_U)):
                sp.dma_start(W[:, s], c.w_in[:, :, col:col + 512]).then_inc(c.w_in_sem[s], 16)
            sp.wait_ge(nb_done, H)
            for h in range(H):
                sp.dma_start(c.sufd[h].rearrange("b (g k) -> (b g) k", k=P),
                             NB[:, h, :]).then_inc(c.sufd_out, 16)

        @block.gpsimd
        def _(pool):
            g = nc.gpsimd
            g.memset(c.ident[:], 0.0).then_inc(ident_zero, 1)
            g.memset(c.ones[:], 1.0).then_inc(ident_zero, 1)
            g.memset(c.neghalf[:], -0.5).then_inc(ident_zero, 1)
            g.memset(c.new_mask[:], BIG).then_inc(ident_zero, 1)
            pool.wait_ge(ident_zero, 4)
            g.affine_select(out=c.ident[:], in_=c.ident[:], compare_op=ALU.not_equal, fill=1.0,
                            base=0, pattern=[[-1, P]], channel_multiplier=1).then_inc(ident_done, 1)
            g.affine_select(out=later, in_=c.ones[:], compare_op=ALU.is_gt, fill=0.0, base=0,
                            pattern=[[-1, P]], channel_multiplier=1).then_inc(const_step, 1)
            pool.wait_ge(const_step, 1)
            g.affine_select(out=later, in_=later, compare_op=ALU.is_gt, fill=0.0, base=PAGES,
                            pattern=[[PAGES, DB], [0, PAGES]],
                            channel_multiplier=-1).then_inc(const_step, 1)
            g.affine_select(out=c.before[:], in_=c.ones[:], compare_op=ALU.is_gt, fill=0.0, base=0,
                            pattern=[[1, P]], channel_multiplier=-1).then_inc(const_step, 1)
            pool.wait_ge(const_step, 3)
            g.tensor_scalar(c.future_b[:], c.before[:], BIG, None, ALU.mult).then_inc(const_step, 1)
            pool.wait_ge(ident_done, 1)
            g.tensor_copy(c.ident_b[:], c.ident[:]).then_inc(const_step, 1)
            pool.wait_ge(pidx_in, 16)
            g.indirect_dma_start(out=view(c, A_AT, P * H), out_offset=None, in_=c.cache_logf,
                                 in_offset=bass.IndirectOffsetOnAxis(ap=pidx, axis=0)
                                 ).then_inc(logf_in, 16)
            for t in range(NT):
                pool.wait_ge(ms_done, t + 1)
                g.tensor_tensor(c.stat[:, 2, t:t + 1], c.stat[:, 1, t:t + 1],
                                c.neghalf[:, 0:1], ALU.pow).then_inc(rstd_done, 1)

        @block.scalar
        def _(act):
            s = nc.scalar
            act.dma_start(pidx, c.page_rows).then_inc(pidx_in, 16)
            with nc.allow_non_contiguous_dma(reason="gains by partition, once"):
                act.dma_start(c.g_mix[:], c.norm_mix_g).then_inc(gains_in, 16)
                act.dma_start(c.g_moe[:], c.norm_moe_g).then_inc(c.consts_in, 16)
                act.dma_start(c.g_ple[:], c.norm_ple_g).then_inc(c.consts_in, 16)
            act.dma_start(c.w_route[:, :, 0:NG], c.w_router_group).then_inc(c.consts_in, 16)
            act.dma_start(c.w_route[:, :, NG:], c.w_router_expert).then_inc(c.consts_in, 16)
            act.dma_start(c.b_route[:, 0:NG], c.b_router_group).then_inc(c.consts_in, 16)
            act.dma_start(c.b_route[:, NG:], c.b_router_expert).then_inc(c.consts_in, 16)
            for t in range(NT):
                act.wait_ge(rstd_done, t + 1)
                s.activation(X[:, t, :], X[:, t, :], ACT.Copy,
                             scale=c.stat[:, 2, t:t + 1]).then_inc(xn_done, 1)

        @block.tensor
        def _(pe):
            pe.wait_ge(ident_done, 1)
            for t in range(NT):
                pe.wait_ge(xn_done, t + 1)
                for half in range(2):
                    n = 2 * t + half
                    if n >= 4:
                        pe.wait_ge(ht_done, n - 3)
                    for k in range(4):
                        mm = nc.tensor.transpose(c.bank[n % 4][:, k * P:(k + 1) * P],
                                                 X[:, t, (4 * half + k) * P:(4 * half + k + 1) * P],
                                                 c.ident[:])
                    mm.then_inc(tr_done, 1)
            pe.wait_ge(scan_done, H)
            pe.wait_ge(const_step, 2)
            nc.tensor.matmul(c.bank[4][:, 0:H], later, PRE[:, :, P - 1], start=True,
                             stop=True).then_inc(carry_mm, 1)

        @block.vector
        def _(dve):
            v = nc.vector
            v.memset(view(c, Q_AT, NT, D)[NS:P, NP, :], 0.0).then_inc(pad_zero, 1)

            def evac(n):
                t, half = n // 2, n % 2
                dve.wait_ge(tr_done, n + 1)
                v.tensor_tensor(HT[:, t, 4 * half:4 * half + 4, :],
                                c.bank[n % 4][:, :].rearrange("p (k n) -> p k n", k=4),
                                bcast(c.g_mix[:, 4 * half:4 * half + 4], P),
                                ALU.mult).then_inc(ht_done, 1)

            for t in range(NT):
                dve.wait_ge(x_in[t], 16)
                if t == NP:
                    dve.wait_ge(pad_zero, 1)
                if t:
                    dve.wait_ge(ss_done, t)
                v.tensor_tensor_reduce(junk, X[:, t, :], X[:, t, :], 1.0, 0.0, ALU.mult, ALU.add,
                                       c.stat[:, 0, t:t + 1]).then_inc(ss_done, 1)
                dve.wait_ge(ss_done, t + 1)
                v.tensor_scalar(c.stat[:, 1, t:t + 1], c.stat[:, 0, t:t + 1], 1.0 / D, EPS,
                                ALU.mult, ALU.add).then_inc(ms_done, 1)
                if t == 0:
                    dve.wait_ge(gains_in, 16)
                if t >= 2:
                    evac(2 * t - 4)
                    evac(2 * t - 3)
            for n in range(2 * NT - 4, 2 * NT):
                evac(n)
            own = view(c, A_AT + 3300, DT)[0:NS]
            dve.wait_ge(const_step, 3)
            v.tensor_reduce(own, c.before[0:NS, 0:NS].rearrange("p (h j) -> p j h", h=H), AX.X,
                            ALU.add).then_inc(dve_step, 1)
            dve.wait_ge(dve_step, 1)
            dve.wait_ge(ident_zero, 4)
            v.tensor_scalar(c.new_mask[:, NS:NS + DT], own, own[:, 0:1], BIG, ALU.subtract,
                            ALU.mult).then_inc(dve_step, 1)
            dve.wait_ge(logf_in, 16)
            for h in range(H):
                v.tensor_tensor_scan(PRE[:, h, :], c.ones[:], LF[:, :, h], 0.0, ALU.mult,
                                     ALU.add).then_inc(scan_done, 1)
            dve.wait_ge(scan_done, H)
            dve.wait_ge(carry_mm, 1)
            v.tensor_tensor(carry, c.bank[4][:, 0:H], PRE[:, :, P - 1], ALU.add).then_inc(carry_done, 1)
            dve.wait_ge(carry_done, 1)
            for h in range(H):
                v.tensor_scalar(NB[:, h, :], PRE[:, h, :], carry[:, h:h + 1], None,
                                ALU.subtract).then_inc(nb_done, 1)


def stage_project(nc, c):
    HT = view(c, HT_AT, NT, KD, P)
    W = view(c, W_AT, 4, KD, 512)
    QT = view(c, Q_AT, NT, NPAIR, P)
    KT = view(c, K_AT, NT, NPAIR, P)
    K_ROWS = view(c, A_AT, NT, WA)
    V_ROWS = view(c, V_AT, NT, WA)
    t0 = T_AT
    w_f = view(c, t0, KD, H)
    t0 += KD * H
    b_f = view(c, t0, H)
    t0 += H
    Z, AZ, Y, U, L, LF = [view(c, t0 + i * NT * H, NT, H) for i in range(6)]
    t0 += 6 * NT * H
    assert t0 <= T_END
    LT = view(c, K_AT, NT * P)[0:H]
    CT = view(c, K_AT + NT * P, NT * P)[0:H]
    reset = view(c, K_AT + 2 * NT * P, NS)[0:H]
    wf_in, bf_in = c.sem("wf_in"), c.sem("bf_in")
    q_mm, q_ev_a, q_ev_v = c.sem("q_mm"), c.sem("q_ev_act"), c.sem("q_ev_dve")
    f_mm, row_mm, row_free = c.sem("f_mm"), c.sem("row_mm"), c.sem("row_free")
    fstep, fact, lt_tr, lt_ev = c.sem("f_step"), c.sem("f_act"), c.sem("lt_tr"), c.sem("lt_ev")
    c.out_rows, c.scan_out = c.kept_sem("out_rows"), c.kept_sem("scan_out")
    scanned = c.sem("scanned")
    kt_tr, kt_ev = c.sem("kt_tr"), c.sem("kt_ev")
    reset_done = c.sem("reset_done")
    c.w_vb_in, c.ws_in, c.bs_in, c.ln_in = (c.kept_sem(n) for n in
                                           ("w_vb_in", "ws_in", "bs_in", "ln_in"))
    pieces = [(0, 4), (4, 8), (8, 9)]
    q_groups = [(a, b, j) for a, b in pieces for j in range(NPAIR)]
    NQ = len(q_groups)
    with nc.Block() as block:
        @block.sync
        def _(sp):
            sp.wait_ge(q_mm, NQ)
            sp.dma_start(W[:, 0], c.w_in[:, :, OFF_VB:OFF_VB + 512]).then_inc(c.w_vb_in, 16)
            for n, (out_p, out_s) in enumerate(((c.new_v_p, c.new_v_s), (c.new_k_p, c.new_k_s))):
                src = (V_ROWS, K_ROWS)[n]
                sp.wait_ge(row_free, 3 + NT * (n + 1))
                sp.dma_start(out_p.rearrange("(t p) d -> p t d", p=P), src[:, 0:NP, :]).then_inc(c.out_rows, 16)
                sp.dma_start(out_s, src[0:NS, NP, :]).then_inc(c.out_rows, 16)

        @block.gpsimd
        def _(pool):
            g = nc.gpsimd
            pool.dma_start(w_f, c.w_in[:, :, OFF_F:OFF_F + H]).then_inc(wf_in, 16)
            pool.dma_start(b_f, c.b_f).then_inc(bf_in, 16)
            g.memset(reset, 1.0).then_inc(reset_done, 1)
            pool.wait_ge(reset_done, 1)
            g.memset(reset.rearrange("p (b t) -> p b t", t=DT)[:, :, 0:1], 0.0).then_inc(reset_done, 1)

        @block.tensor
        def _(pe):
            mm = nc.tensor.matmul
            pe.wait_ge(c.w_in_sem[0], 16)
            for n, (a, b, j) in enumerate(q_groups):
                if n >= 4:
                    pe.wait_ge(q_ev_a if n % 2 else q_ev_v, (n - 4) // 2 + 1)
                for k in range(KD):
                    last = mm(c.bank[n % 4][:, 0:(b - a) * P], W[:, 0, k, j * P:(j + 1) * P],
                              HT[:, a:b, k, :], start=(k == 0), stop=(k == KD - 1))
                last.then_inc(q_mm, 1)
            pe.wait_ge(wf_in, 16)
            for t in range(NT):
                for k in range(KD):
                    last = mm(c.bank[7][:, t * H:(t + 1) * H], HT[:, t, k, :], w_f[:, k, :],
                              start=(k == 0), stop=(k == KD - 1))
            last.then_inc(f_mm, 1)
            for s in range(1, 4):
                pe.wait_ge(c.w_in_sem[s], 16)
            with pe.Fori(0, 3) as n:
                for t in range(NT):
                    pe.wait_ge(row_free, n * NT + (t + 1))
                    for k in range(KD):
                        last = mm(c.bank[4 + t % 3][:, :], HT[:, t, k, :],
                                  c.arena[:, bass.ds(W_AT + WBLK + k * 512 + n * WBLK, 512)],
                                  start=(k == 0), stop=(k == KD - 1))
                    last.then_inc(row_mm, 1)
            pe.wait_ge(q_ev_a, NQ // 2)
            pe.wait_ge(fstep, 8)
            for t in range(NT):
                tr = nc.tensor.transpose(c.bank[t // 4][0:H, (t % 4) * P:(t % 4 + 1) * P], LF[:, t, :],
                                         c.ident[:])
            tr.then_inc(lt_tr, 1)
            pe.wait_ge(row_free, 3 + 3 * NT)
            for t in range(NT):
                if t >= 2:
                    pe.wait_ge(kt_ev, t - 1)
                for j in range(NPAIR):
                    tr = nc.tensor.transpose(c.bank[4 + t % 2][:, j * P:(j + 1) * P],
                                             K_ROWS[:, t, j * P:(j + 1) * P], c.ident[:])
                tr.then_inc(kt_tr, 1)

        @block.scalar
        def _(act):
            s = nc.scalar
            for n, (a, b, j) in enumerate(q_groups):
                if n % 2:
                    act.wait_ge(q_mm, n + 1)
                    s.activation(QT[:, a:b, j, :], c.bank[n % 4][:, 0:(b - a) * P].rearrange(
                        "p (t n) -> p t n", n=P), ACT.Copy, scale=-SCALE).then_inc(q_ev_a, 1)
            act.wait_ge(fstep, 2)
            s.activation(Y, AZ, ACT.Exp).then_inc(fact, 1)
            act.wait_ge(fstep, 3)
            s.activation(L, U, ACT.Ln).then_inc(fact, 1)
            act.wait_ge(fstep, 8)
            act.dma_start(c.new_lf_p.rearrange("(t p) h -> p t h", p=P), LF[:, 0:NP, :]).then_inc(c.out_rows, 16)
            act.dma_start(c.new_lf_s, LF[0:NS, NP, :]).then_inc(c.out_rows, 16)
            act.wait_ge(scanned, 2)
            act.dma_start(c.cum_d, CT[:, 0:SEQ + NS]).then_inc(c.scan_out, 16)

        @block.vector
        def _(dve):
            v = nc.vector
            dve.sem_inc(row_free, 3)
            for n, (a, b, j) in enumerate(q_groups):
                if n % 2 == 0:
                    dve.wait_ge(q_mm, n + 1)
                    v.tensor_scalar(QT[:, a:b, j, :], c.bank[n % 4][:, 0:(b - a) * P].rearrange(
                        "p (t n) -> p t n", n=P), -SCALE, None, ALU.mult).then_inc(q_ev_v, 1)
            dve.wait_ge(f_mm, 1)
            dve.wait_ge(bf_in, 16)
            v.tensor_tensor(Z, c.bank[7][:, 0:NT * H].rearrange("p (t h) -> p t h", h=H),
                            b_f.unsqueeze(1).to_broadcast([P, NT, H]), ALU.add).then_inc(fstep, 1)
            dve.wait_ge(fstep, 1)
            v.scalar_tensor_tensor(out=AZ, in0=Z, scalar=-1.0, in1=Z, op0=ALU.mult,
                                   op1=ALU.min).then_inc(fstep, 1)
            dve.wait_ge(fact, 1)
            v.tensor_scalar(U, Y, 1.0, None, ALU.add).then_inc(fstep, 1)
            dve.wait_ge(fstep, 3)
            v.scalar_tensor_tensor(out=Y, in0=U, scalar=-1.0, in1=Y, op0=ALU.add,
                                   op1=ALU.subtract).then_inc(fstep, 1)
            dve.wait_ge(fact, 2)
            v.reciprocal(AZ, U).then_inc(fstep, 1)
            dve.wait_ge(fstep, 5)
            v.tensor_tensor(Y, Y, AZ, ALU.mult).then_inc(fstep, 1)
            dve.wait_ge(fstep, 6)
            v.tensor_tensor(Y, Y, L, ALU.subtract).then_inc(fstep, 1)
            dve.wait_ge(fstep, 7)
            v.scalar_tensor_tensor(out=LF, in0=Z, scalar=0.0, in1=Y, op0=ALU.min,
                                   op1=ALU.add).then_inc(fstep, 1)
            dve.wait_ge(c.sufd_out, 16 * H)
            with dve.Fori(0, 3) as n:
                for t in range(NT):
                    dve.wait_ge(row_mm, n * NT + (t + 1))
                    v.tensor_scalar(c.arena[:, bass.ds(V_AT + t * WA + n * (NT * WA), WA)],
                                    c.bank[4 + t % 3][:, :], 1.0, None, ALU.mult).then_inc(row_free, 1)
            dve.wait_ge(lt_tr, 1)
            for a, b in pieces:
                v.tensor_copy(LT[:, a * P:b * P], c.bank[a // 4][0:H, 0:(b - a) * P]).then_inc(lt_ev, 1)
            dve.wait_ge(lt_ev, 3)
            dve.wait_ge(reset_done, 2)
            v.tensor_tensor_scan(CT[:, 0:SEQ], c.ones[0:H, 0:1].to_broadcast([H, SEQ]), LT[:, 0:SEQ], 0.0, ALU.mult,
                                 ALU.add).then_inc(scanned, 1)
            v.tensor_tensor_scan(CT[:, SEQ:SEQ + NS], reset, LT[:, SEQ:SEQ + NS], 0.0, ALU.mult,
                                 ALU.add).then_inc(scanned, 1)
            dve.wait_ge(c.scan_out, 16)
            for t in range(NT):
                dve.wait_ge(kt_tr, t + 1)
                v.tensor_copy(KT[:, t], c.bank[4 + t % 2][:, :].rearrange("p (j n) -> p j n", n=P)
                              ).then_inc(kt_ev, 1)


def stage_mlp(nc, c):
    HT = view(c, HT_AT, NT, KD, P)
    W = view(c, W_AT, 4, KD, 512)
    U_ROWS = view(c, B_AT, NT, WA)
    BT = view(c, B_AT, NT, KF, P)
    at = W_AT + WBLK
    raw_p, raw_s = view(c, at, H, P), view(c, at + 1024, H, P)
    mix_p, mix_s = view(c, at + 2048, H, P), view(c, at + 3072, H, P)
    at += WBLK
    ln_g, ln_b = view(c, at, WA), view(c, at + WA, WA)
    bias_p, bias_s = view(c, at + 1024, H), view(c, at + 1032, H)
    at += 1040
    VG = view(c, at, 3, WA)
    VN = view(c, at + 3 * WA, 2, WA)
    BO = view(c, at + 5 * WA, 2, WA)
    SV = view(c, at + 7 * WA, 2, WA)
    bn = view(c, T_AT, NT, 6)
    mv = view(c, T_AT + 6 * NT, NT, 4)
    zero_done, raw_in, ln_in, masked = c.sem("mlp_zero"), c.sem("mlp_raw_in"), c.sem("mlp_ln_in"), c.sem("mlp_masked")
    mix_tr, mix_ev = c.sem("mix_tr"), c.sem("mix_ev")
    vb_mm, gelu_v, gelu_u = c.sem("vb_mm"), c.sem("gelu_v"), c.sem("gelu_u")
    stat_step, rstd_done, normed, gained, vn_done = (c.sem("ln_stat"), c.sem("ln_rstd"), c.sem("ln_normed"),
                                                     c.sem("ln_gained"), c.sem("vn_done"))
    sv_mm, sv_ev, bo_done, bt_tr, bt_ev = (c.sem("sv_mm"), c.sem("sv_ev"), c.sem("bo_done"),
                                           c.sem("bt_tr"), c.sem("bt_ev"))
    small = "rows of a few elements, once"
    with nc.Block() as block:
        @block.sync
        def _(sp):
            sp.dma_start(raw_p, c.w_spatial.rearrange("g t s -> t g s")).then_inc(raw_in, 16)
            sp.dma_start(ln_g, c.ln_v_g).then_inc(ln_in, 16)
            sp.dma_start(ln_b, c.ln_v_b).then_inc(ln_in, 16)
            sp.wait_ge(zero_done, 2)
            with nc.allow_non_contiguous_dma(reason=small):
                sp.dma_start(bias_p, c.b_spatial.rearrange("g t -> t g")).then_inc(raw_in, 16)
                for b in range(DB):
                    r = slice(b * DT, (b + 1) * DT)
                    sp.dma_start(raw_s[r, :, r], c.w_spatial[:, 0:DT, 0:DT].rearrange("g t s -> t g s")
                                 ).then_inc(raw_in, 16)
                    sp.dma_start(bias_s[r, :], c.b_spatial[:, 0:DT].rearrange("g t -> t g")).then_inc(raw_in, 16)
            sp.wait_ge(vn_done, NT)
            sp.dma_start(c.new_cv_s, VN[0:NS, NP % 2, :]).then_inc(c.out_rows, 16)

        @block.gpsimd
        def _(pool):
            g = nc.gpsimd
            g.memset(raw_s, 0.0).then_inc(zero_done, 1)
            g.memset(bias_s, 0.0).then_inc(zero_done, 1)
            pool.wait_ge(raw_in, 16 * (2 + 2 * DB))
            for m in (raw_p, raw_s):
                g.affine_select(out=m, in_=m, compare_op=ALU.is_ge, fill=0.0, base=0,
                                pattern=[[0, H], [-1, P]], channel_multiplier=1).then_inc(masked, 1)
            pool.wait_ge(ln_in, 32)
            for t in range(NT):
                pool.wait_ge(stat_step, 3 * t + 3)
                g.tensor_tensor(mv[:, t, 3:4], mv[:, t, 2:3], c.neghalf[:, 0:1], ALU.pow).then_inc(rstd_done, 1)
                pool.wait_ge(normed, t + 1)
                g.tensor_tensor(VG[:, t % 3, :], VG[:, t % 3, :], ln_g, ALU.mult).then_inc(gained, 1)
                pool.wait_ge(gained, t + 1)
                if t >= 2:
                    pool.wait_ge(sv_mm, t - 1)
                g.tensor_tensor(VN[:, t % 2, :], VG[:, t % 3, :], ln_b, ALU.add).then_inc(vn_done, 1)

        @block.tensor
        def _(pe):
            mm = nc.tensor.matmul
            pe.wait_ge(c.w_vb_in, 16)

            def spatial(t):
                pe.wait_ge(vn_done, t + 1)
                if t >= 1:
                    pe.wait_ge(sv_ev, t)
                w = mix_p if t < NP else mix_s
                for gr in range(H):
                    last = mm(c.bank[4][:, gr * DH:(gr + 1) * DH], w[:, gr, :],
                              VN[:, t % 2, gr * DH:(gr + 1) * DH], start=True, stop=True)
                last.then_inc(sv_mm, 1)

            def turn(t):
                pe.wait_ge(bo_done, t + 1)
                if t >= 2:
                    pe.wait_ge(bt_ev, t - 1)
                for j in range(KF):
                    last = nc.tensor.transpose(c.bank[5 + t % 2][:, j * P:(j + 1) * P],
                                               BO[:, t % 2, j * P:(j + 1) * P], c.ident[:])
                last.then_inc(bt_tr, 1)

            for t in range(NT + 3):
                if t < NT:
                    if t >= 2:
                        pe.wait_ge(gelu_v, t - 1)
                    for k in range(KD):
                        last = mm(c.bank[t % 2][:, :], HT[:, t, k, :], W[:, 0, k, :], start=(k == 0),
                                  stop=(k == KD - 1))
                    last.then_inc(vb_mm, 1)
                if t == 0:
                    pe.wait_ge(masked, 2)
                    for n, (raw, half) in enumerate(((raw_p, 0), (raw_p, 1), (raw_s, 0), (raw_s, 1))):
                        if n >= 2:
                            pe.wait_ge(mix_ev, n - 1)
                        for gr in range(4):
                            last = nc.tensor.transpose(c.bank[2 + n % 2][:, gr * P:(gr + 1) * P],
                                                       raw[:, 4 * half + gr, :], c.ident[:])
                        last.then_inc(mix_tr, 1)
                    pe.wait_ge(mix_ev, 4)
                if 2 <= t < NT + 2:
                    spatial(t - 2)
                if t >= 3:
                    turn(t - 3)

        @block.scalar
        def _(act):
            s = nc.scalar
            for t in range(NT):
                s.activation(U_ROWS[:, t, :], U_ROWS[:, t, :], ACT.Gelu_apprx_tanh).then_inc(gelu_u, 1)
                act.wait_ge(vb_mm, t + 1)
                if t >= 3:
                    act.wait_ge(vn_done, t - 2)
                s.activation(VG[:, t % 3, :], c.bank[t % 2][:, :], ACT.Gelu_apprx_tanh).then_inc(gelu_v, 1)

        @block.vector
        def _(dve):
            v = nc.vector
            for n in range(4):
                dve.wait_ge(mix_tr, n + 1)
                dst = (mix_p, mix_p, mix_s, mix_s)[n]
                v.tensor_copy(dst[:, 4 * (n % 2):4 * (n % 2) + 4, :],
                              c.bank[2 + n % 2][:, :].rearrange("p (g n) -> p g n", n=P)).then_inc(mix_ev, 1)

            def combine(t):
                dve.wait_ge(sv_mm, t + 1)
                dve.wait_ge(raw_in, 16 * (2 + 2 * DB))
                if t >= 2:
                    dve.wait_ge(bo_done, t - 1)
                bias = bias_p if t < NP else bias_s
                v.tensor_tensor(SV[:, t % 2, :].rearrange("p (g d) -> p g d", d=DH),
                                c.bank[4][:, :].rearrange("p (g d) -> p g d", d=DH),
                                bcast(bias, DH), ALU.add).then_inc(sv_ev, 1)
                dve.wait_ge(sv_ev, t + 1)
                dve.wait_ge(gelu_u, t + 1)
                if t >= 2:
                    dve.wait_ge(bt_tr, t - 1)
                v.tensor_tensor(BO[:, t % 2, :], SV[:, t % 2, :], U_ROWS[:, t, :], ALU.mult).then_inc(bo_done, 1)

            def keep(t):
                dve.wait_ge(bt_tr, t + 1)
                v.tensor_copy(BT[:, t], c.bank[5 + t % 2][:, :].rearrange("p (j n) -> p j n", n=P)).then_inc(bt_ev, 1)

            for t in range(NT + 3):
                if t < NT:
                    dve.wait_ge(gelu_v, t + 1)
                    v.bn_stats(bn[:, t, :], VG[:, t % 3, :]).then_inc(stat_step, 1)
                    dve.wait_ge(stat_step, 3 * t + 1)
                    v.bn_aggr(mv[:, t, 0:2], bn[:, t, :]).then_inc(stat_step, 1)
                    dve.wait_ge(stat_step, 3 * t + 2)
                    v.tensor_scalar(mv[:, t, 2:3], mv[:, t, 1:2], EPS, None, ALU.add).then_inc(stat_step, 1)
                    dve.wait_ge(rstd_done, t + 1)
                    v.tensor_scalar(VG[:, t % 3, :], VG[:, t % 3, :], mv[:, t, 0:1], mv[:, t, 3:4],
                                    ALU.subtract, ALU.mult).then_inc(normed, 1)
                if 2 <= t < NT + 2:
                    combine(t - 2)
                if t >= 3:
                    keep(t - 3)


def stage_prompt_attention(nc, c):
    QT = view(c, Q_AT, NT, NPAIR, P)
    KT = view(c, K_AT, NT, NPAIR, P)
    AR = view(c, A_AT, NT, WA)
    AT = view(c, A_AT, NT, NPAIR, P)
    QS, KS = view(c, W_AT, NP, P), view(c, W_AT + SEQ, NP, P)
    BH = view(c, W_AT + 2 * SEQ, 2, SEQ)
    S = view(c, W_AT + 4 * SEQ, 2, SEQ)
    PT = view(c, W_AT + 6 * SEQ, 2, NP, P)
    pace = view(c, T_AT + 10, 2 * NP)
    low, total, inv = view(c, T_AT, 2), view(c, T_AT + 2, 4), view(c, T_AT + 6, 4)
    bh_in = [c.sem("bias_in0"), c.sem("bias_in1")]
    staged, s_mm, ttr, exps = c.sem("staged"), c.sem("s_mm"), c.sem("s_biased"), c.sem("exps")
    tr_a, tr_b, ev_a, ev_b = c.sem("p_tr_a"), c.sem("p_tr_b"), c.sem("p_ev_a"), c.sem("p_ev_b")
    pv, rc, norm = c.sem("pv"), c.sem("inv_done"), c.sem("attn_rows")
    at_tr, at_ev = c.sem("at_tr"), c.sem("at_ev")
    zeros = view(c, T_AT + 1024, D)
    blank, c.blank_out = c.sem("blank"), c.kept_sem("blank_out")
    N = 2 * NP

    def late(n):
        return (n // NP) * (NP - 4) + max(n % NP - 4, 0)

    NB = late(N)
    with nc.Block() as block:
        @block.sync
        def _(sp):
            sp.wait_ge(blank, 1)
            sp.dma_start(c.y_d[NE * P:].rearrange("(n p) d -> p n d", p=P),
                         zeros.unsqueeze(1).to_broadcast([P, NOVER, D])).then_inc(c.blank_out, 16)
            sp.wait_ge(c.scan_out, 16)
            for hl in range(2):
                sp.dma_start(BH[:, hl, :], c.cum_d[hl:hl + 1, 0:SEQ].to_broadcast([P, SEQ])).then_inc(bh_in[hl], 16)
            with sp.Fori(0, NPAIR - 1) as pr:
                for hl in range(2):
                    sp.wait_ge(ttr, pr * N + NP * (hl + 1))
                    sp.dma_start(BH[:, hl, :], c.cum_d[bass.ds(2 * pr + 2 + hl, 1), 0:SEQ].to_broadcast([P, SEQ])
                                 ).then_inc(bh_in[hl], 16)
            sp.wait_ge(c.blank_out, 16)

        @block.gpsimd
        def _(pool):
            nc.gpsimd.memset(zeros, 0.0).then_inc(blank, 1)

        @block.tensor
        def _(pe):
            mm = nc.tensor.matmul
            with pe.Fori(0, NPAIR) as pr:
                pe.wait_ge(staged, 2 * pr + 2)

                def scores(n):
                    hl, i = n // NP, n % NP
                    r = slice(hl * DH, (hl + 1) * DH)
                    if n >= 2:
                        pe.wait_ge(ttr, pr * N + (n - 1))
                    for half in range(i // 4 + 1):
                        a, b = 4 * half, min(4 * half + 4, i + 1)
                        mm(c.bank[2 * (n % 2) + half][:, 0:(b - a) * P], QS[r, i, :], KS[r, a:b, :],
                           start=True, stop=False, skip_group_check=True)
                    last = mm(c.bank[2 * (n % 2) + i // 4][:, (i % 4) * P:(i % 4 + 1) * P], c.ident_b[:],
                              c.future_b[:], start=False, stop=True, skip_group_check=True)
                    last.then_inc(s_mm, 1)

                def turn(n):
                    i = n % NP
                    pe.wait_ge(exps, pr * N + (n + 1))
                    if n >= 1:
                        pe.wait_ge(ev_a, pr * N + n)
                    for k in range(min(i + 1, 4)):
                        last = nc.tensor.transpose(c.bank[4][:, k * P:(k + 1) * P], S[:, n % 2, k * P:(k + 1) * P],
                                                   c.ident[:])
                    last.then_inc(tr_a, 1)
                    if i >= 4:
                        if late(n) >= 1:
                            pe.wait_ge(ev_b, pr * NB + late(n))
                        for k in range(4, i + 1):
                            last = nc.tensor.transpose(c.bank[5][:, (k - 4) * P:(k - 3) * P],
                                                       S[:, n % 2, k * P:(k + 1) * P], c.ident[:])
                        last.then_inc(tr_b, 1)

                def weigh(n):
                    hl, i = n // NP, n % NP
                    pe.wait_ge(ev_a, pr * N + (n + 1))
                    if n >= 2:
                        pe.wait_ge(norm, pr * N + (n - 1))
                    for k in range(i + 1):
                        if k == 4:
                            pe.wait_ge(ev_b, pr * NB + (late(n) + 1))
                        last = mm(c.bank[6 + n % 2][:, 0:DH], PT[:, n % 2, k, :],
                                  c.arena[:, bass.ds(V_AT + k * WA + hl * DH + pr * (2 * DH), DH)],
                                  start=(k == 0), stop=(k == i))
                    last.then_inc(pv, 1)

                for n in range(N + 2):
                    if n < N:
                        scores(n)
                    if 1 <= n < N + 1:
                        turn(n - 1)
                    if n >= 2:
                        weigh(n - 2)
            for t in range(NP):
                if t == 0:
                    pe.wait_ge(norm, NPAIR * N)
                if t >= 2:
                    pe.wait_ge(at_ev, t - 1)
                for j in range(NPAIR):
                    last = nc.tensor.transpose(c.bank[t % 2][:, j * P:(j + 1) * P], AR[:, t, j * P:(j + 1) * P],
                                               c.ident[:])
                last.then_inc(at_tr, 1)

        @block.scalar
        def _(act):
            s = nc.scalar
            with act.Fori(0, NPAIR) as pr:
                for n in range(N + 1):
                    if n < N:
                        i = n % NP
                        act.wait_ge(ttr, pr * N + (n + 1))
                        w = (i + 1) * P
                        s.activation(S[:, n % 2, 0:w], S[:, n % 2, 0:w], ACT.Exp, bias=low[:, n % 2:n % 2 + 1],
                                     scale=-1.0, accum_out=total[:, n % 4:n % 4 + 1]).then_inc(exps, 1)
                    if n >= 1:
                        m, i = n - 1, (n - 1) % NP
                        act.wait_ge(tr_a, pr * N + (m + 1))
                        if m >= 2:
                            act.wait_ge(pv, pr * N + (m - 1))
                        w = min(i + 1, 4)
                        s.activation(PT[:, m % 2, 0:w, :], c.bank[4][:, 0:w * P].rearrange("p (k n) -> p k n", n=P),
                                     ACT.Copy).then_inc(ev_a, 1)

        @block.vector
        def _(dve):
            v = nc.vector
            dve.wait_ge(c.out_rows, 16 * 7)
            with dve.Fori(0, NPAIR) as pr:
                for dst, src in ((QS, QT), (KS, KT)):
                    v.tensor_scalar(dst.rearrange("p t (o n) -> p t o n", o=1), src[:, 0:NP, bass.ds(pr, 1), :], 1.0,
                                    None, ALU.mult).then_inc(staged, 1)

                def bias(n):
                    hl, i = n // NP, n % NP
                    if i == 0:
                        dve.wait_ge(bh_in[hl], pr * 16 + 16)
                    dve.wait_ge(s_mm, pr * N + (n + 1))
                    w = (i + 1) * P
                    if n >= 2:
                        dve.wait_ge(tr_a, pr * N + (n - 1))
                        if (n - 2) % NP >= 4:
                            dve.wait_ge(tr_b, pr * NB + (late(n - 2) + 1))
                    v.memset(pace[:, n:n + 1], 0.0)
                    two = c.psum_pair(n % 2)
                    v.tensor_tensor_reduce(S[:, n % 2, 0:w], two[:, 0:w], BH[:, hl, 0:w], 1.0, 3e38, ALU.add,
                                           ALU.min, low[:, n % 2:n % 2 + 1]).then_inc(ttr, 1)

                def keep_late(n):
                    i = n % NP
                    if i >= 4:
                        dve.wait_ge(tr_b, pr * NB + (late(n) + 1))
                        if n >= 2:
                            dve.wait_ge(pv, pr * N + (n - 1))
                        v.tensor_copy(PT[:, n % 2, 4:i + 1, :],
                                      c.bank[5][:, 0:(i - 3) * P].rearrange("p (k n) -> p k n", n=P)).then_inc(ev_b, 1)

                def scale(n):
                    hl, i = n // NP, n % NP
                    dve.wait_ge(pv, pr * N + (n + 1))
                    v.reciprocal(inv[:, n % 4:n % 4 + 1], total[:, n % 4:n % 4 + 1]).then_inc(rc, 1)
                    dve.wait_ge(rc, pr * N + (n + 1))
                    v.tensor_scalar(c.arena[:, bass.ds(A_AT + i * WA + hl * DH + pr * (2 * DH), DH)],
                                    c.bank[6 + n % 2][:, 0:DH], inv[:, n % 4:n % 4 + 1], None,
                                    ALU.mult).then_inc(norm, 1)

                for n in range(N + 2):
                    if n < N:
                        bias(n)
                    if 1 <= n < N + 1:
                        keep_late(n - 1)
                    if n >= 2:
                        scale(n - 2)
            for t in range(NP):
                dve.wait_ge(at_tr, t + 1)
                v.tensor_copy(AT[:, t], c.bank[t % 2][:, :].rearrange("p (j n) -> p j n", n=P)).then_inc(at_ev, 1)


def stage_sample_attention(nc, c):
    QT8 = view(c, Q_AT + NP * WA, NPAIR, P)
    KT8 = view(c, K_AT + NP * WA, NPAIR, P)
    V8 = view(c, V_AT + NP * WA, WA)
    AT8 = view(c, A_AT + NP * WA, NPAIR, P)
    R = NS
    CH = 4
    NCH = PAGES // CH
    U = NCH * NPAIR
    KC = view(c, W_AT, NCH, CH, WA)
    VC = view(c, W_AT + NCH * CH * WA, NCH, CH, WA)
    KTS = view(c, Q_AT, NPAIR, CH * P)
    PTS = view(c, Q_AT + 2048, PAGES, R)
    OS = view(c, Q_AT + 3072, WA)[0:R]
    low5 = view(c, Q_AT + 3584, 2, NCH + 1)[0:R]
    low = view(c, Q_AT + 3600, 2)[0:R]
    sums, inv = view(c, Q_AT + 3604, 2, 2)[0:R], view(c, Q_AT + 3610, 2)[0:R]
    PNS = view(c, Q_AT + 3620, R)[0:R]
    pace = view(c, Q_AT + 3700, 2, NCH + 1)[0:R]
    pages = view(c, Q_AT + 3720, DB * PAGES).bitcast(I32)[0:1]
    S = view(c, K_AT, 2, PAST)[0:R]
    NBIAS = view(c, V_AT, 2, PAST)[0:R]
    QB = view(c, T_AT, 2, 320)
    SN = view(c, T_AT + 640, 2, R)[0:R]
    NBN = view(c, T_AT + 768, 2, R)[0:R]
    CN = view(c, T_AT + 896, R)[0:R]
    pages_in, cn_in, bias_in = c.sem("pages_in"), c.sem("cn_in"), [c.sem(f"suffix_in{p}") for p in range(2)]
    k_in, v_in = [c.sem(f"k_in{i}") for i in range(NCH)], [c.sem(f"v_in{i}") for i in range(NCH)]
    v_used, zeroed = c.sem("v_used"), c.sem("qb_zeroed")
    k_tr, kt_v, kt_a = c.sem("k_tr"), c.sem("kt_dve"), c.sem("kt_act")
    qb_done, nbn_done = c.sem("qb_done"), c.sem("nbn_done")
    unit_mm, sn_mm = c.sem("unit_mm"), c.sem("own_s_mm")
    ttr, ttr_own, low_done, exps = c.sem("page_biased"), c.sem("own_biased"), c.sem("low_done"), c.sem("page_exps")
    p_tr, own_tr, p_ev_a, p_ev_v, own_ev = (c.sem("pp_tr"), c.sem("own_tr"), c.sem("pp_ev_act"), c.sem("pp_ev_dve"),
                                            c.sem("own_ev"))
    pv, inv_step, os_done, ot_tr, ot_ev = (c.sem("page_pv"), c.sem("inv_step"), c.sem("os_done"), c.sem("ot_tr"),
                                           c.sem("ot_ev"))

    def batches(eng, step, tail):
        step(0, 0, 0)
        step(1, 1, 1)
        with eng.Fori(0, (DB - 2) // 2) as i:
            step(2 * i + 2, 0, 2)
            step(2 * i + 3, 1, 2)
        tail()

    with nc.Block() as block:
        @block.sync
        def _(sp):
            sp.dma_start(pages, c.page_table.rearrange("(o b) g -> o (b g)", o=1)).then_inc(pages_in, 16)
            for h in range(H):
                sp.dma_start(CN[h * DT:(h + 1) * DT, :],
                             c.cum_d[h:h + 1, SEQ:].to_broadcast([DT, NS])).then_inc(cn_in, 16)
            sp.wait_ge(pages_in, 16)
            sp.wait_ge(c.sufd_out, 16 * H)

            def step(b, p, has):
                if has >= 2:
                    sp.wait_ge(ttr, NCH * b - NCH)
                for h in range(H):
                    sp.dma_start(NBIAS[h * DT:(h + 1) * DT, p, :],
                                 c.sufd[h, bass.ds(b, 1), :].to_broadcast([DT, PAST])).then_inc(bias_in[p], 16)
                for ch in range(NCH):
                    if has >= 1:
                        sp.wait_ge(k_tr, U * b + (NPAIR * (ch + 1) - U))
                    for g in range(CH):
                        page = sp.value_load(pages[0:1, bass.ds(b * PAGES + (ch * CH + g), 1)], min_val=0,
                                             max_val=c.n_pool - 1)
                        sp.dma_start(KC[:, ch, g, :], c.cache_k[bass.ds(page * P, P), :]).then_inc(k_in[ch], 16)

            batches(sp, step, lambda: None)

        @block.gpsimd
        def _(pool):
            g_ = nc.gpsimd
            g_.memset(QB, 0.0).then_inc(zeroed, 1)
            g_.memset(AT8, 0.0).then_inc(zeroed, 1)
            pool.wait_ge(pages_in, 16)

            def step(b, p, has):
                for ch in range(NCH):
                    if has >= 1:
                        pool.wait_ge(v_used, NCH * b + (ch + 1 - NCH))
                    for g in range(CH):
                        page = pool.value_load(pages[0:1, bass.ds(b * PAGES + (ch * CH + g), 1)], min_val=0,
                                               max_val=c.n_pool - 1)
                        pool.dma_start(VC[:, ch, g, :], c.cache_v[bass.ds(page * P, P), :]).then_inc(v_in[ch], 16)

            batches(pool, step, lambda: None)

        @block.tensor
        def _(pe):
            mm, tp = nc.tensor.matmul, nc.tensor.transpose

            def unit_turn(b, u, has):
                ch, j = u // NPAIR, u % NPAIR
                if j == 0:
                    pe.wait_ge(k_in[ch], 64 * b + 64)
                if has or u >= 2:
                    pe.wait_ge(kt_a if j % 2 else kt_v, (U // 2) * b + u // 2)
                for g in range(CH):
                    last = tp(c.bank[2 + j % 2][:, g * P:(g + 1) * P], KC[:, ch, g, j * P:(j + 1) * P], c.ident[:])
                last.then_inc(k_tr, 1)

            def unit_score(b, p, u, has):
                ch, j = u // NPAIR, u % NPAIR
                pe.wait_ge(kt_a if j % 2 else kt_v, (U // 2) * b + (u // 2 + 1))
                if j == 0 and (has or ch >= 2):
                    pe.wait_ge(ttr, NCH * b + (ch - 1))
                last = mm(c.bank[ch % 2][0:R, :], QB[:, p, j * R:(j + 1) * R], KTS[:, j, :], start=(j == 0),
                          stop=(j == NPAIR - 1))
                last.then_inc(unit_mm, 1)

            def own_scores(b, p, has):
                pe.wait_ge(qb_done, 2 * b + 2)
                if has >= 2:
                    pe.wait_ge(own_ev, b - 1)
                for j in range(NPAIR):
                    last = mm(c.bank[7][0:R, 448:512], QB[:, p, j * R:(j + 1) * R], KT8[:, j, 0:R], start=(j == 0),
                              stop=(j == NPAIR - 1))
                last.then_inc(sn_mm, 1)

            def may_turn(b, first):
                pe.wait_ge(exps, 2 * b + 2)
                if not first:
                    pe.wait_ge(p_ev_a, b)
                    pe.wait_ge(p_ev_v, b)
                    pe.wait_ge(ot_ev, 2 * b)

            def turn(b, p):
                for g in range(PAGES):
                    last = tp(c.bank[4 + g // 8][:, (g % 8) * R:(g % 8 + 1) * R], S[:, p, g * P:(g + 1) * P],
                              c.ident[0:R, 0:R])
                last.then_inc(p_tr, 1)
                tp(c.bank[7][0:R, 0:R], SN[:, p, :], c.ident[0:R, 0:R]).then_inc(own_tr, 1)

            def weigh(b, first):
                pe.wait_ge(p_ev_a, b + 1)
                if not first:
                    pe.wait_ge(os_done, b)
                for ch in range(NCH):
                    pe.wait_ge(v_in[ch], 64 * b + 64)
                    if ch == 2:
                        pe.wait_ge(own_ev, b + 1)
                        pe.wait_ge(p_ev_v, b + 1)
                    for g in range(CH):
                        last = mm(c.bank[6][0:R, :], PTS[:, ch * CH + g, :], VC[:, ch, g, :], start=(ch + g == 0),
                                  stop=False)
                    last.then_inc(v_used, 1)
                mm(c.bank[6][0:R, :], PNS, V8[0:R, :], start=False, stop=True).then_inc(pv, 1)

            def out_turn(b):
                for j in range(NPAIR):
                    last = tp(c.bank[7][:, j * R:(j + 1) * R], OS[:, j * P:(j + 1) * P], c.ident[0:R, 0:R])
                last.then_inc(ot_tr, 1)

            def step(b, p, has):
                own_scores(b, p, has)
                for u in range(U + 2):
                    if u == NPAIR - 1 and has >= 2:
                        pe.wait_ge(ttr_own, b + 1)
                        pe.wait_ge(os_done, b - 1)
                    if u == 3 * NPAIR - 1 and has >= 1:
                        if has < 2:
                            pe.wait_ge(ttr_own, b + 1)
                        may_turn(b - 1, has < 2)
                    if u < U:
                        unit_turn(b, u, has)
                    if u >= 2:
                        unit_score(b, p, u - 2, has)
                    if u == NPAIR - 1 and has >= 2:
                        out_turn(b - 2)
                    if u == 3 * NPAIR - 1 and has >= 1:
                        turn(b - 1, 1 - p)
                if has >= 1:
                    weigh(b - 1, has < 2)

            def tail():
                pe.wait_ge(os_done, DB - 1)
                out_turn(DB - 2)
                may_turn(DB - 1, False)
                turn(DB - 1, (DB - 1) % 2)
                weigh(DB - 1, False)
                pe.wait_ge(os_done, DB)
                out_turn(DB - 1)

            batches(pe, step, tail)

        @block.scalar
        def _(act):
            s = nc.scalar

            def unit_copy(b, u, has):
                j = u % NPAIR
                act.wait_ge(k_tr, U * b + (u + 1))
                if has or u >= NPAIR:
                    act.wait_ge(unit_mm, U * b + (u + 1 - NPAIR))
                s.activation(KTS[:, j, :], c.bank[2 + j % 2][:, :], ACT.Copy).then_inc(kt_a, 1)

            def weights_copy(b, first):
                act.wait_ge(p_tr, b + 1)
                if not first:
                    act.wait_ge(pv, b)
                s.activation(PTS[:, 0:8, :], c.bank[4][:, :].rearrange("p (g r) -> p g r", r=R),
                             ACT.Copy).then_inc(p_ev_a, 1)

            def exp(b, p):
                act.wait_ge(low_done, b + 1)
                s.activation(S[:, p, :], S[:, p, :], ACT.Exp, bias=low[:, p:p + 1], scale=-1.0,
                             accum_out=sums[:, p, 0:1]).then_inc(exps, 1)
                s.activation(SN[:, p, :], SN[:, p, :], ACT.Exp, bias=low[:, p:p + 1], scale=-1.0,
                             accum_out=sums[:, p, 1:2]).then_inc(exps, 1)

            def step(b, p, has):
                for u in range(U):
                    if u == 3 * NPAIR and has >= 1:
                        weights_copy(b - 1, has < 2)
                    if u % 2:
                        unit_copy(b, u, has)
                exp(b, p)

            batches(act, step, lambda: weights_copy(DB - 1, False))

        @block.vector
        def _(dve):
            v = nc.vector

            def spread(b, p):
                for half in range(2):
                    r = slice(half * DH, (half + 1) * DH)
                    v.tensor_scalar(qb_cells(p, half), QT8[r, :, bass.ds(b * DT, DT)], 1.0, None, ALU.mult).then_inc(qb_done, 1)
                v.tensor_tensor(NBN[:, p, :], CN, c.new_mask[:, bass.ds(NS - b * DT, NS)],
                                ALU.add).then_inc(nbn_done, 1)

            def qb_cells(p, half):
                r = slice(half * DH, (half + 1) * DH)
                flat = c.arena[r, T_AT + p * 320 + half * DT:T_AT + p * 320 + half * DT + 4 * 80]
                return flat.rearrange("p (j n) -> p j n", n=80)[:, :, 0:DT]

            def own_bias(b, p):
                dve.wait_ge(sn_mm, b + 1)
                dve.wait_ge(nbn_done, b + 1)
                v.memset(pace[:, p, NCH:NCH + 1], 0.0)
                v.tensor_tensor_reduce(SN[:, p, :], c.bank[7][0:R, 448:512], NBN[:, p, :], 1.0, 3e38, ALU.add,
                                       ALU.min, low5[:, p, NCH:NCH + 1]).then_inc(ttr_own, 1)

            def bias(b, p, ch):
                if ch == 0:
                    dve.wait_ge(bias_in[p], 64 * b + (2 - p) * 64)
                dve.wait_ge(unit_mm, U * b + NPAIR * (ch + 1))
                v.memset(pace[:, p, ch:ch + 1], 0.0)
                v.tensor_tensor_reduce(S[:, p, ch * 512:(ch + 1) * 512], c.bank[ch % 2][0:R, :],
                                       NBIAS[:, p, ch * 512:(ch + 1) * 512], 1.0, 3e38, ALU.add, ALU.min,
                                       low5[:, p, ch:ch + 1]).then_inc(ttr, 1)

            def unit_copy(b, u, has):
                j = u % NPAIR
                dve.wait_ge(k_tr, U * b + (u + 1))
                if has or u >= NPAIR:
                    dve.wait_ge(unit_mm, U * b + (u + 1 - NPAIR))
                v.tensor_copy(KTS[:, j, :], c.bank[2 + j % 2][:, :]).then_inc(kt_v, 1)

            def weights_copy(b):
                dve.wait_ge(p_tr, b + 1)
                v.tensor_copy(PTS[:, 8:16, :], c.bank[5][:, :].rearrange("p (g r) -> p g r", r=R)).then_inc(p_ev_v, 1)
                dve.wait_ge(own_tr, b + 1)
                v.tensor_copy(PNS, c.bank[7][0:R, 0:R]).then_inc(own_ev, 1)

            def out_rows(b, p, first):
                dve.wait_ge(exps, 2 * b + 2)
                v.tensor_tensor(inv[:, p:p + 1], sums[:, p, 0:1], sums[:, p, 1:2], ALU.add).then_inc(inv_step, 1)
                dve.wait_ge(inv_step, 2 * b + 1)
                v.reciprocal(inv[:, p:p + 1], inv[:, p:p + 1]).then_inc(inv_step, 1)
                dve.wait_ge(inv_step, 2 * b + 2)
                dve.wait_ge(pv, b + 1)
                if not first:
                    dve.wait_ge(ot_tr, b)
                v.tensor_scalar(OS, c.bank[6][0:R, :], inv[:, p:p + 1], None, ALU.mult).then_inc(os_done, 1)

            def out_cells(b):
                dve.wait_ge(ot_tr, b + 1)
                for half in range(2):
                    r = slice(half * DH, (half + 1) * DH)
                    cells = c.bank[7][r, half * DT:half * DT + 4 * 80].rearrange("p (j n) -> p j n", n=80)[:, :, 0:DT]
                    v.tensor_scalar(AT8[r, :, bass.ds(b * DT, DT)], cells, 1.0, None, ALU.mult).then_inc(ot_ev, 1)

            def step(b, p, has):
                own_bias(b, p)
                spread(b + 1, 1 - p)
                for u in range(U):
                    if u == NPAIR and has >= 2:
                        out_cells(b - 2)
                    if u == 3 * NPAIR and has >= 1:
                        weights_copy(b - 1)
                    if u % 2 == 0:
                        unit_copy(b, u, has)
                    if u % NPAIR == 0 and u:
                        bias(b, p, u // NPAIR - 1)
                bias(b, p, NCH - 1)
                dve.wait_ge(ttr, NCH * b + NCH)
                dve.wait_ge(ttr_own, b + 1)
                v.tensor_reduce(low[:, p:p + 1], low5[:, p, :], AX.X, ALU.min).then_inc(low_done, 1)
                if has >= 1:
                    out_rows(b - 1, 1 - p, has < 2)

            def tail():
                out_cells(DB - 2)
                weights_copy(DB - 1)
                out_rows(DB - 1, (DB - 1) % 2, False)
                out_cells(DB - 1)

            dve.wait_ge(zeroed, 2)
            dve.wait_ge(cn_in, 16 * H)
            spread(0, 0)
            batches(dve, step, tail)


def stage_merge(nc, c):
    HT = view(c, HT_AT, NT, KD, P)
    AT, BT = view(c, A_AT, NT, KF, P), view(c, B_AT, NT, KF, P)
    MT = view(c, Q_AT, NT, KD, P)
    SGA, SGB, M = view(c, T_AT, 2, 512), view(c, T_AT + 1024, 2, 512), view(c, T_AT + 2048, 2, 512)
    GA, GB, UP = (W_AT, 3 * WBLK), (W_AT + WBLK, V_AT - W_AT - WBLK), (W_AT + 2 * WBLK, -2 * WBLK)
    ga_in, gb_in, up_in = c.sem("ga_in"), c.sem("gb_in"), c.sem("up_in")
    half_mm, b_mm, ga_mm, gb_mm = c.sem("half_mm"), c.sem("up_mm"), c.sem("ga_mm"), c.sem("gb_mm")
    sig_a, sig_b, prod_a, prod_b, m_done = (c.sem("sig_a"), c.sem("sig_b"), c.sem("prod_a"), c.sem("prod_b"),
                                            c.sem("m_done"))
    m_tr, m_ev = c.sem("m_tr"), c.sem("m_ev")
    c.wo_in = c.kept_sem("wo_in")

    def block_at(at, second):
        return view(c, at[0] + at[1] * second, KD, 512)

    with nc.Block() as block:
        @block.sync
        def _(sp):
            def load(at, second, col, sem):
                sp.dma_start(block_at(at, second), c.w_in[:, :, col + 512 * second:col + 512 * second + 512]
                             ).then_inc(sem, 16)

            def load_up(second):
                for n, w in enumerate((c.w_up_a, c.w_up_b)):
                    sp.dma_start(block_at(UP, second)[:, n * KF:(n + 1) * KF, :],
                                 w[:, :, 512 * second:512 * second + 512]).then_inc(up_in, 16)

            load(GA, 0, OFF_GA, ga_in)
            load(GB, 0, OFF_GB, gb_in)
            load_up(0)
            sp.wait_ge(ga_in, 16)
            load(GA, 1, OFF_GA, ga_in)
            sp.wait_ge(gb_in, 16)
            load(GB, 1, OFF_GB, gb_in)
            sp.wait_ge(b_mm, NT)
            load_up(1)
            for n in range(2):
                sp.dma_start(view(c, W_AT + (1 + n) * WBLK, KD, 512), c.w_o[:, :, 512 * n:512 * n + 512]
                             ).then_inc(c.wo_in, 16)

        @block.tensor
        def _(pe):
            mm = nc.tensor.matmul
            with pe.Fori(0, 2) as half:
                def product(bank, lhs, at, k0, n):
                    for k in range(n):
                        last = mm(c.bank[bank][:, :], lhs[:, k, :],
                                  c.arena[:, bass.ds(at[0] + (k0 + k) * 512 + half * at[1], 512)],
                                  start=(k == 0), stop=(k == n - 1))
                    return last

                def turn(t):
                    pe.wait_ge(m_done, half * NT + (t + 3))
                    pe.wait_ge(m_ev, half * NT + (t + 1))
                    for j in range(4):
                        last = nc.tensor.transpose(c.bank[4][:, j * P:(j + 1) * P], M[:, t % 2, j * P:(j + 1) * P],
                                                   c.ident[:])
                    last.then_inc(m_tr, 1)

                pe.wait_ge(ga_in, half * 16 + 16)
                for t in range(NT):
                    pe.wait_ge(sig_a, half * NT + (t + 1))
                    product(0, HT[:, t], GA, 0, KD).then_inc(ga_mm, 1)
                    if t == 0:
                        pe.wait_ge(gb_in, half * 16 + 16)
                    pe.wait_ge(sig_b, half * NT + (t + 1))
                    product(1, HT[:, t], GB, 0, KD).then_inc(gb_mm, 1)
                    if t == 0:
                        pe.wait_ge(up_in, half * 32 + 32)
                    else:
                        turn(t - 1)
                    pe.wait_ge(prod_b, half * NT + (t + 1))
                    product(2, AT[:, t], UP, 0, KF)
                    product(3, BT[:, t], UP, KF, KF).then_inc(b_mm, 1)
                turn(NT - 1)

        @block.scalar
        def _(act):
            s = nc.scalar
            act.sem_inc(sig_a, 1)
            act.sem_inc(sig_b, 1)
            with act.Fori(0, 2) as half:
                for t in range(NT):
                    act.wait_ge(ga_mm, half * NT + (t + 1))
                    act.wait_ge(m_done, half * NT + (t + 1))
                    s.activation(SGA[:, t % 2, :], c.bank[0][:, :], ACT.Sigmoid).then_inc(sig_a, 1)
                    act.wait_ge(gb_mm, half * NT + (t + 1))
                    s.activation(SGB[:, t % 2, :], c.bank[1][:, :], ACT.Sigmoid).then_inc(sig_b, 1)

        @block.vector
        def _(dve):
            v = nc.vector
            dve.sem_inc(prod_b, 1)
            dve.sem_inc(m_done, 2)
            dve.sem_inc(m_ev, 1)
            with dve.Fori(0, 2) as half:
                def keep(t):
                    dve.wait_ge(m_tr, half * NT + (t + 1))
                    v.tensor_scalar(c.arena[:, bass.ds(Q_AT + t * D + half * 512, 512)], c.bank[4][:, :], 1.0, None,
                                    ALU.mult).then_inc(m_ev, 1)

                for t in range(NT):
                    if t >= 1:
                        keep(t - 1)
                    dve.wait_ge(b_mm, half * NT + (t + 1))
                    dve.wait_ge(sig_a, half * NT + (t + 2))
                    dve.wait_ge(sig_b, half * NT + (t + 2))
                    v.tensor_tensor(SGA[:, t % 2, :], SGA[:, t % 2, :], c.bank[2][:, :], ALU.mult).then_inc(prod_a, 1)
                    v.tensor_tensor(SGB[:, t % 2, :], SGB[:, t % 2, :], c.bank[3][:, :], ALU.mult).then_inc(prod_b, 1)
                    dve.wait_ge(prod_a, half * NT + (t + 1))
                    dve.wait_ge(prod_b, half * NT + (t + 2))
                    v.tensor_tensor(M[:, t % 2, :], SGA[:, t % 2, :], SGB[:, t % 2, :], ALU.add).then_inc(m_done, 1)
                keep(NT - 1)


def stage_out(nc, c):
    MT = view(c, Q_AT, NT, KD, P)
    X1 = view(c, HT_AT, NT, D)
    WO = view(c, W_AT + WBLK, 2, KD, 512)
    XR = view(c, W_AT + 3 * WBLK, 3, D)
    H2 = view(c, W_AT, 3, D)
    HT2 = view(c, T_AT, 2, KD, P)
    junk = view(c, T_AT + 2 * D, D)
    x_in = [c.sem(f"xr_in{i}") for i in range(3)]
    h2_out = c.h2_out = [c.kept_sem(f"h2_out{i}") for i in range(3)]
    pad, xo_mm, x1_done, ss_done, ms_done, rstd = (c.sem("xr_pad"), c.sem("xo_mm"), c.sem("x1_done"), c.sem("x1_ss"),
                                                   c.sem("x1_ms"), c.sem("x1_rstd"))
    h2_done, h2_tr, h2_ev, c.logit_mm = c.sem("h2_done"), c.sem("h2_tr"), c.sem("h2_ev"), c.kept_sem("logit_mm")
    zero, c.table_out = c.sem("table_zero"), c.kept_sem("table_out")
    zeros = view(c, Q_AT - 300, SLOTS // P).bitcast(I32)
    moe_weights(c)
    with nc.Block() as block:
        @block.sync
        def _(sp):
            for t in range(NT):
                if t >= 3:
                    sp.wait_ge(x1_done, 2 * (t - 2))
                src = c.x_prompt[t * P:(t + 1) * P, :] if t < NP else c.x_sample
                n = src.shape[0]
                sp.dma_start(XR[0:n, t % 3, :], src).then_inc(x_in[t % 3], 16)
            for kind, e in (("gate", 0), ("up", 0), ("gate", 1)):
                c.load_expert(sp, kind, e, e % 2)
            sp.wait_ge(zero, 1)
            sp.dma_start(c.slot_tok.rearrange("(p n) o -> p (n o)", p=P), zeros).then_inc(c.table_out, 16)

        @block.gpsimd
        def _(pool):
            g = nc.gpsimd
            g.memset(zeros, 0).then_inc(zero, 1)
            for t in range(NT):
                if t == NP:
                    pool.wait_ge(x1_done, 2 * (NP - 2))
                    pool.wait_ge(rstd, NP)
                    g.memset(XR[NS:P, NP % 3, :], 0.0).then_inc(pad, 1)
                pool.wait_ge(ms_done, t + 1)
                g.tensor_tensor(c.stat[:, 2, t:t + 1], c.stat[:, 1, t:t + 1], c.neghalf[:, 0:1],
                                ALU.pow).then_inc(rstd, 1)

        @block.scalar
        def _(act):
            s = nc.scalar
            for t in range(NT):
                act.wait_ge(rstd, t + 1)
                if t >= 3:
                    act.wait_ge(h2_out[t % 3], 16 * (t // 3))
                    act.wait_ge(h2_tr, 2 * (t - 2))
                s.activation(H2[:, t % 3, :], X1[:, t, :], ACT.Copy, scale=c.stat[:, 2, t:t + 1]).then_inc(h2_done, 1)
                act.wait_ge(h2_done, t + 1)
                act.dma_start(c.h2_d[t * P:(t + 1) * P, :], H2[:, t % 3, :]).then_inc(h2_out[t % 3], 16)

        @block.tensor
        def _(pe):
            mm = nc.tensor.matmul

            def turn(t):
                pe.wait_ge(h2_done, t + 1)
                for half in range(2):
                    if t >= 1:
                        pe.wait_ge(h2_ev, 2 * t - 1 + half)
                    for k in range(4):
                        last = nc.tensor.transpose(c.bank[4 + half][:, k * P:(k + 1) * P],
                                                   H2[:, t % 3, (4 * half + k) * P:(4 * half + k + 1) * P], c.ident[:])
                    last.then_inc(h2_tr, 1)

            def logits(t):
                pe.wait_ge(h2_ev, 2 * t + 2)
                for k in range(KD):
                    last = mm(c.bank[6][:, t * (NG + NE):(t + 1) * (NG + NE)], HT2[:, t % 2, k, :], c.w_route[:, k, :],
                              start=(k == 0), stop=(k == KD - 1))
                last.then_inc(c.logit_mm, 1)

            pe.wait_ge(c.wo_in, 32)
            pe.wait_ge(c.consts_in, 16 * 6)
            for t in range(NT + 2):
                if t < NT:
                    for half in range(2):
                        if t >= 2:
                            pe.wait_ge(x1_done, 2 * t - 3 + half)
                        for k in range(KD):
                            last = mm(c.bank[2 * (t % 2) + half][:, :], MT[:, t, k, :], WO[:, half, k, :],
                                      start=(k == 0), stop=(k == KD - 1))
                        last.then_inc(xo_mm, 1)
                        if half == 0 and t >= 1:
                            turn(t - 1)
                            if t >= 2:
                                logits(t - 2)
                elif t == NT:
                    turn(t - 1)
                    logits(t - 2)
                else:
                    logits(t - 2)

        @block.vector
        def _(dve):
            v = nc.vector

            def keep(t):
                for half in range(2):
                    dve.wait_ge(h2_tr, 2 * t + half + 1)
                    if t >= 2:
                        dve.wait_ge(c.logit_mm, t - 1)
                    v.tensor_tensor(HT2[:, t % 2, 4 * half:4 * half + 4, :],
                                    c.bank[4 + half][:, :].rearrange("p (k n) -> p k n", n=P),
                                    bcast(c.g_moe[:, 4 * half:4 * half + 4], P), ALU.mult).then_inc(h2_ev, 1)

            for t in range(NT + 1):
                if t < NT:
                    dve.wait_ge(x_in[t % 3], 16 * (t // 3 + 1))
                    if t == NP:
                        dve.wait_ge(pad, 1)
                    for half in range(2):
                        cols = slice(512 * half, 512 * half + 512)
                        dve.wait_ge(xo_mm, 2 * t + half + 1)
                        v.tensor_tensor(X1[:, t, cols], c.bank[2 * (t % 2) + half][:, :], XR[:, t % 3, cols],
                                        ALU.add).then_inc(x1_done, 1)
                    dve.wait_ge(x1_done, 2 * t + 2)
                    v.tensor_tensor_reduce(junk, X1[:, t, :], X1[:, t, :], 1.0, 0.0, ALU.mult, ALU.add,
                                           c.stat[:, 0, t:t + 1]).then_inc(ss_done, 1)
                    dve.wait_ge(ss_done, t + 1)
                    v.tensor_scalar(c.stat[:, 1, t:t + 1], c.stat[:, 0, t:t + 1], 1.0 / D, EPS, ALU.mult,
                                    ALU.add).then_inc(ms_done, 1)
                if t >= 1:
                    keep(t - 1)


MOE_GATE = (V_AT, V_AT + 2 * WBLK)
MOE_UP = (V_AT + WBLK, Q_AT + WBLK)
MOE_DOWN = (Q_AT, W_AT)
MOE_AT = W_AT + WBLK


def moe_weights(c):
    c.expert_in = {k: [c.kept_sem(f"w_{k}{j}") for j in range(2)] for k in ("gate", "up", "down")}
    at = {"gate": MOE_GATE, "up": MOE_UP, "down": MOE_DOWN}
    c.expert_w = {k: [view(c, at[k][j], KD, FF) if k != "down" else view(c, at[k][j], KF, D) for j in range(2)]
                  for k in at}
    src = {"gate": (c.w_gate, D), "up": (c.w_up, D), "down": (c.w_down, FF)}

    def load(eng, kind, e, j):
        w, rows_ = src[kind]
        eng.dma_start(c.expert_w[kind][j], w[bass.ds(e * rows_, rows_), :].rearrange("(k p) n -> p k n", p=P)
                      ).then_inc(c.expert_in[kind][j], 16)

    c.load_expert = load


def stage_route(nc, c):
    at = [MOE_AT]

    def take(*dims):
        v = view(c, at[0], *dims)
        at[0] += int(np.prod(dims))
        return v

    K = NG + NE
    LG = take(NT, K)
    gmax, gsel, pg, m1, i1, m2, i2, w0, e1, e2 = [take(NT) for _ in range(10)]
    GD, eqg, oneg = take(NT, NG), take(NT, NG), take(NT, NG)
    ES, E2, eq8, one8, tmp8 = [take(NT, NEG) for _ in range(5)]
    OH1, OH2, OHS, POS, TMP = [take(NT, NE) for _ in range(5)]
    BASE = take(NT + 1, NE)
    FAR = take(NT, NE)
    jump = take(NE)
    iota = take(NE)
    slot0 = take(NE)
    step_no = take(NOVER)
    tok_f, pos_f = take(NT), take(2, NT)
    tok_i = take(NT).bitcast(I32)
    tab_i, tab_f, idx_f = take(P).bitcast(I32), take(P), take(NE)
    extra, cum, over = take(NE), take(NE), take(NOVER + 1)
    pick = take(NOVER, NE)
    assert at[0] <= Q_AT
    OFFI = 99.0
    c.w_tok = view(c, T_AT, 2, NT)
    c.slot_i = view(c, T_AT + 20, 2, NT).bitcast(I32)
    c.idx = view(c, T_AT + 40, NE)
    c.over_i = view(c, T_AT + 80, NOVER + 1).bitcast(I32)
    step, aux = c.sem("route_step"), c.sem("route_aux")
    ge, ve, rank_mm, slots, scat, tab_in, tab_tr = (c.sem("g_exp"), c.sem("v_exp"), c.sem("rank_mm"),
                                                    c.sem("slots_done"), c.sem("scattered"), c.sem("table_in"),
                                                    c.sem("table_tr"))
    gd_done, vd_done, oh_done, tabf, c.idx_done = (c.sem("gd_done"), c.sem("vd_done"), c.sem("oh_done"),
                                                   c.sem("tab_f"), c.kept_sem("idx_done"))
    with nc.Block() as block:
        @block.sync
        def _(sp):
            c.load_expert(sp, "down", 0, 0)
            c.load_expert(sp, "up", 1, 1)

        @block.gpsimd
        def _(pool):
            g = nc.gpsimd
            g.iota(iota, pattern=[[1, NE]], base=-99, channel_multiplier=0,
                   allow_small_or_imprecise_dtypes=True).then_inc(aux, 1)
            g.iota(slot0, pattern=[[P, NE]], base=0, channel_multiplier=0,
                   allow_small_or_imprecise_dtypes=True).then_inc(aux, 1)
            g.iota(step_no, pattern=[[1, NOVER]], base=0, channel_multiplier=0,
                   allow_small_or_imprecise_dtypes=True).then_inc(aux, 1)
            g.iota(tok_i, pattern=[[P, NT]], base=0, channel_multiplier=1).then_inc(aux, 1)
            pool.wait_ge(c.table_out, 16)
            pool.wait_ge(aux, 4)
            pool.wait_ge(slots, 1)
            for t in range(NT):
                n = P if t < NP else NS
                for r in range(2):
                    g.indirect_dma_start(out=c.slot_tok, in_=tok_i[0:n, t:t + 1], in_offset=None,
                                         out_offset=bass.IndirectOffsetOnAxis(ap=c.slot_i[0:n, r, t:t + 1], axis=0)
                                         ).then_inc(scat, 16)
            pool.wait_ge(scat, 16 * 2 * NT)
            pool.dma_start(tab_i[0:NE], c.slot_tok[0:NE * P].rearrange("(e r) o -> e (r o)", e=NE)
                           ).then_inc(tab_in, 16)

        @block.tensor
        def _(pe):
            pe.wait_ge(oh_done, 1)
            flat = OHS.rearrange("p t e -> p (t e)")
            nc.tensor.matmul(c.bank[0][:, 0:NT * NE], c.before[:], flat, start=True, stop=True)
            nc.tensor.matmul(c.bank[1][:, 0:NT * NE], c.ones[:], flat, start=True, stop=True).then_inc(rank_mm, 1)
            pe.wait_ge(tabf, 1)
            nc.tensor.transpose(c.bank[2][:, 0:NE], tab_f[0:NE], c.ident[0:NE, 0:NE]).then_inc(tab_tr, 1)

        @block.scalar
        def _(act):
            act.wait_ge(gd_done, 1)
            nc.scalar.activation(GD, GD, ACT.Exp).then_inc(ge, 1)
            act.wait_ge(vd_done, 1)
            nc.scalar.activation(m2, m2, ACT.Exp).then_inc(ve, 1)

        @block.vector
        def _(dve):
            v = nc.vector
            count = [0]

            def do(ins):
                count[0] += 1
                ins.then_inc(step, 1)
                dve.wait_ge(step, count[0])

            def over_tiles(row, n):
                return row.unsqueeze(1).to_broadcast([row.shape[0], NT, n])

            def tt(out, a, b, op):
                do(v.tensor_tensor(out, a, b, op))

            def first_max(vals, n, top, where, eq, one):
                do(v.tensor_reduce(top, vals, AX.X, ALU.max))
                tt(eq, vals, bcast(top, n), ALU.is_equal)
                tt(eq, eq, over_tiles(iota[:, 0:n], n), ALU.mult)
                do(v.tensor_reduce(where, eq, AX.X, ALU.min))
                tt(one, over_tiles(iota[:, 0:n], n), bcast(where, n), ALU.is_equal)

            dve.wait_ge(c.logit_mm, NT)
            dve.wait_ge(aux, 3)
            tt(LG, c.bank[6][:, 0:NT * K].rearrange("p (t k) -> p t k", k=K), over_tiles(c.b_route[:], K), ALU.add)
            G = LG[:, :, 0:NG]
            first_max(G, NG, gmax, gsel, eqg, oneg)
            v.tensor_tensor(GD, G, bcast(gmax, NG), ALU.subtract).then_inc(gd_done, 1)
            for g in range(NG):
                dst = ES if g == 0 else tmp8
                tt(dst, LG[:, :, NG + g * NEG:NG + (g + 1) * NEG], oneg[:, :, g:g + 1].to_broadcast([P, NT, NEG]),
                   ALU.mult)
                if g:
                    tt(ES, ES, tmp8, ALU.add)
            first_max(ES, NEG, m1, i1, eq8, one8)
            do(v.scalar_tensor_tensor(out=E2, in0=one8, scalar=-BIG, in1=ES, op0=ALU.mult, op1=ALU.add))
            first_max(E2, NEG, m2, i2, eq8, one8)
            dve.wait_ge(step, count[0])
            v.tensor_tensor(m2, m2, m1, ALU.subtract).then_inc(vd_done, 1)
            for i, e in ((i1, e1), (i2, e2)):
                do(v.scalar_tensor_tensor(out=e, in0=gsel, scalar=float(NEG), in1=i, op0=ALU.mult, op1=ALU.add))
                do(v.tensor_scalar(e, e, NEG * OFFI, None, ALU.add))
            for e, one in ((e1, OH1), (e2, OH2)):
                tt(one, over_tiles(iota, NE), bcast(e, NE), ALU.is_equal)
                do(v.memset(one[NS:P, NP, :], 0.0))
            dve.wait_ge(step, count[0])
            v.tensor_tensor(OHS, OH1, OH2, ALU.add).then_inc(oh_done, 1)
            dve.wait_ge(ge, 1)
            do(v.tensor_reduce(pg, GD, AX.X, ALU.add))
            dve.wait_ge(ve, 1)
            do(v.tensor_scalar(w0, m2, 1.0, None, ALU.add))
            tt(w0, w0, pg, ALU.mult)
            do(v.reciprocal(c.w_tok[:, 0, :], w0))
            tt(c.w_tok[:, 1, :], c.w_tok[:, 0, :], m2, ALU.mult)
            dve.wait_ge(rank_mm, 1)
            do(v.memset(BASE[:, 0, :], 0.0))
            for t in range(NT):
                tt(BASE[:, t + 1, :], BASE[:, t, :], c.bank[1][:, t * NE:(t + 1) * NE], ALU.add)
            tt(POS, BASE[:, 0:NT, :], c.bank[0][:, 0:NT * NE].rearrange("p (t e) -> p t e", e=NE), ALU.add)
            cnt = BASE[:, NT, :]
            do(v.tensor_scalar(extra, cnt, float(BLK), None, ALU.is_gt))
            for b in range(2, TOK // BLK):
                do(v.scalar_tensor_tensor(out=extra, in0=cnt, scalar=float(b * BLK), in1=extra, op0=ALU.is_gt,
                                          op1=ALU.add))
            do(v.tensor_tensor_scan(cum, c.ones[:, 0:NE], extra, 0.0, ALU.mult, ALU.add))
            tt(jump, cum, extra, ALU.subtract)
            do(v.tensor_scalar(jump, jump, float(P), float(NE * P - BLK), ALU.mult, ALU.add))
            tt(jump, jump, slot0, ALU.subtract)
            do(v.tensor_scalar(FAR, POS, float(BLK), None, ALU.is_ge))
            tt(FAR, FAR, over_tiles(jump, NE), ALU.mult)
            tt(POS, POS, over_tiles(slot0, NE), ALU.add)
            tt(POS, POS, FAR, ALU.add)
            for r, one in enumerate((OH1, OH2)):
                tt(TMP, POS, one, ALU.mult)
                do(v.tensor_reduce(pos_f[:, r, :], TMP, AX.X, ALU.add))
            v.tensor_copy(c.slot_i, pos_f).then_inc(slots, 1)
            tt(pick[0:1], cum[0:1].unsqueeze(1).to_broadcast([1, NOVER, NE]),
               bcast(step_no[0:1], NE), ALU.is_le)
            do(v.tensor_reduce(over[0:1, 0:NOVER], pick[0:1], AX.X, ALU.add))
            do(v.tensor_copy(over[0:1, NOVER:], cum[0:1, NE - 1:NE]))
            v.tensor_copy(c.over_i[0:1], over[0:1])
            dve.wait_ge(tab_in, 16)
            v.tensor_copy(tab_f[0:NE], tab_i[0:NE]).then_inc(tabf, 1)
            dve.wait_ge(tab_tr, 1)
            v.tensor_copy(c.idx, c.bank[2][:, 0:NE]).then_inc(c.idx_done, 1)


def stage_moe(nc, c):
    XG = view(c, MOE_AT, 2, D)
    XT = view(c, MOE_AT + 2 * D, 2, KD, P)
    SG, AC = view(c, MOE_AT + 4 * D, FF), view(c, MOE_AT + 4 * D + FF, FF)
    ACT_T = view(c, MOE_AT + 5 * D, KF, P)
    Y = view(c, MOE_AT + 6 * D, 2, D)
    idx_now = view(c, T_AT + 114, 2).bitcast(I32)
    final_weights(c)
    c.final_in = c.kept_sem("final_in")
    gate_ps, up_ps, turn_ps, y_ps, x_ps = c.bank[0], c.bank[1], c.bank[2], c.psum_pair(2), c.psum_pair(3)
    w, w_in = c.expert_w, c.expert_in
    picked, gathers = c.sem("idx_picked"), c.sem("gathers")
    xg_in = [c.sem(f"xg_in{j}") for j in range(2)]
    y_out = c.y_out = [c.kept_sem(f"y_out{j}") for j in range(2)]
    xt_tr, xt_done, gate_mm, silu_done = c.sem("xt_tr"), c.sem("xt_done"), c.sem("gate_mm"), c.sem("silu_done")
    up_mm, act_done, act_tr, act_kept = c.sem("up_mm_e"), c.sem("act_done"), c.sem("act_tr"), c.sem("act_kept")
    down_mm, y_done = c.sem("down_mm"), c.sem("y_done")
    with nc.Block() as block:
        @block.sync
        def _(sp):
            def step(e, j, gate_up=True, down=True, before=True):
                if gate_up:
                    sp.wait_ge(gate_mm, e + 1)
                    c.load_expert(sp, "gate", e + 2, j)
                if down:
                    if before:
                        sp.wait_ge(down_mm, e)
                    c.load_expert(sp, "down", e + 1, 1 - j)
                if before:
                    sp.wait_ge(y_done, e + 1)
                    sp.dma_start(c.y_d[bass.ds((e - 1) * P, P), :], Y[:, 1 - j, :]).then_inc(y_out[1 - j], 16)
                if gate_up:
                    sp.wait_ge(up_mm, e + 1)
                    c.load_expert(sp, "up", e + 2, j)

            for row, src in zip(c.last_rows, (c.b_ple_gate, c.norm_ple_post_g, c.norm_final_g)):
                sp.dma_start(row, src).then_inc(c.final_in, 16)
            sp.dma_start(c.wpg[0], c.w_ple_gate[:, :, 0:512]).then_inc(c.final_in, 16)
            step(0, 0, before=False)
            with sp.Fori(0, NE // 2 - 2) as i:
                step(i * 2 + 1, 1)
                step(i * 2 + 2, 0)
            step(NE - 3, 1)
            step(NE - 2, 0, gate_up=False)
            sp.wait_ge(gate_mm, NE - 1)
            sp.dma_start(c.wpg[1], c.w_ple_gate[:, :, 512:1024]).then_inc(c.final_in, 16)
            sp.wait_ge(up_mm, NE - 1)
            sp.dma_start(c.wpp, c.w_ple_proj).then_inc(c.final_in, 16)
            step(NE - 1, 1, gate_up=False, down=False)
            step(NE, 0, gate_up=False, down=False)

        @block.gpsimd
        def _(pool):
            g = nc.gpsimd

            def gather(e, j):
                pool.wait_ge(picked, e + 1)
                pool.sem_inc(gathers, 1)
                g.indirect_dma_start(out=XG[:, j, :], out_offset=None, in_=c.h2_d,
                                     in_offset=bass.IndirectOffsetOnAxis(ap=idx_now[:, j:j + 1], axis=0)
                                     ).then_inc(xg_in[j], 16)

            for i in range(3):
                pool.wait_ge(c.h2_out[i], 16 * 3)
            for e in range(2):
                gather(e, e)
            with pool.Fori(0, NE // 2 - 1) as i:
                for j in range(2):
                    gather(i * 2 + (j + 2), j)

        @block.tensor
        def _(pe):
            mm = nc.tensor.matmul

            def transposes(e, j, n):
                pe.wait_ge(xg_in[j], n * 16)
                pe.wait_ge(xt_done, e + 1)
                for k in range(KD):
                    last = nc.tensor.transpose(x_ps[:, k * P:(k + 1) * P], XG[:, j, k * P:(k + 1) * P], c.ident[:])
                last.then_inc(xt_tr, 1)

            def product(out, j, kind, ks):
                for k in ks:
                    last = mm(out[:, :], XT[:, j, k, :], w[kind][j][:, k, :], start=(k == 0), stop=(k == KD - 1))
                return last

            def step(e, j, n, more=True, turn=True):
                if more:
                    pe.wait_ge(w_in["gate"][1 - j], (n + j) * 16)
                    pe.wait_ge(silu_done, e + 2)
                    pe.wait_ge(xt_done, e + 3)
                    product(gate_ps, 1 - j, "gate", range(4))
                pe.wait_ge(act_done, e + 2)
                for k in range(KF):
                    last = nc.tensor.transpose(turn_ps[:, k * P:(k + 1) * P], AC[:, k * P:(k + 1) * P], c.ident[:])
                last.then_inc(act_tr, 1)
                if more:
                    product(gate_ps, 1 - j, "gate", range(4, KD)).then_inc(gate_mm, 1)
                pe.wait_ge(w_in["down"][j], n * 16)
                pe.wait_ge(act_kept, e + 1)
                pe.wait_ge(y_done, e + 1)
                for half in range(2):
                    for k in range(KF):
                        last = mm(y_ps[:, half * 512:half * 512 + 512], ACT_T[:, k, :],
                                  w["down"][j][:, k, half * 512:half * 512 + 512], start=(k == 0), stop=(k == KF - 1))
                last.then_inc(down_mm, 1)
                if more:
                    pe.wait_ge(w_in["up"][1 - j], (n + j) * 16)
                    product(up_ps, 1 - j, "up", range(KD)).then_inc(up_mm, 1)
                if turn:
                    transposes(e + 2, j, n + 1)

            transposes(0, 0, 1)
            pe.wait_ge(w_in["gate"][0], 16)
            pe.wait_ge(xt_done, 2)
            product(gate_ps, 0, "gate", range(KD)).then_inc(gate_mm, 1)
            transposes(1, 1, 1)
            pe.wait_ge(w_in["up"][0], 16)
            product(up_ps, 0, "up", range(KD)).then_inc(up_mm, 1)
            with pe.Fori(0, NE // 2 - 1) as i:
                for j in range(2):
                    step(i * 2 + j, j, i + 1)
            step(NE - 2, 0, NE // 2, turn=False)
            step(NE - 1, 1, NE // 2, more=False, turn=False)

        @block.scalar
        def _(act):
            s = nc.scalar

            def silu(e):
                act.wait_ge(gate_mm, e + 1)
                act.wait_ge(act_done, e + 1)
                s.activation(SG, gate_ps[:, :], ACT.Silu).then_inc(silu_done, 1)

            def keep_y(e, j, n):
                act.wait_ge(down_mm, e + 1)
                if not isinstance(n, int) or n:
                    act.wait_ge(y_out[j], n * 16)
                s.activation(Y[:, j, :], y_ps, ACT.Copy).then_inc(y_done, 1)

            act.sem_inc(silu_done, 1)
            act.sem_inc(y_done, 1)
            silu(0)
            silu(1)
            keep_y(0, 0, 0)
            silu(2)
            keep_y(1, 1, 0)
            with act.Fori(1, NE // 2 - 1) as i:
                for j in range(2):
                    silu(i * 2 + (j + 1))
                    keep_y(i * 2 + j, j, i)
            silu(NE - 1)
            keep_y(NE - 2, 0, NE // 2 - 1)
            keep_y(NE - 1, 1, NE // 2 - 1)

        @block.vector
        def _(dve):
            v = nc.vector

            def pick(e, j):
                if not isinstance(e, int):
                    dve.wait_ge(xt_tr, e - 1)
                v.tensor_scalar(idx_now[:, j:j + 1], c.idx[:, bass.ds(e, 1)], 1.0, None, ALU.mult).then_inc(picked, 1)

            def keep_x(e, j):
                dve.wait_ge(xt_tr, e + 1)
                v.tensor_tensor(XT[:, j], x_ps.rearrange("p (k n) -> p k n", n=P), bcast(c.g_moe[:], P),
                                ALU.mult).then_inc(xt_done, 1)

            def multiply(e):
                dve.wait_ge(up_mm, e + 1)
                dve.wait_ge(silu_done, e + 2)
                v.tensor_tensor(AC, SG, up_ps[:, :], ALU.mult).then_inc(act_done, 1)

            def keep_act(e):
                dve.wait_ge(act_tr, e + 1)
                v.tensor_scalar(ACT_T.rearrange("p k n -> p (k n)"), turn_ps[:, :], 1.0, None,
                                ALU.mult).then_inc(act_kept, 1)

            dve.sem_inc(xt_done, 1)
            dve.sem_inc(act_done, 1)
            dve.wait_ge(c.idx_done, 1)
            pick(0, 0)
            pick(1, 1)
            keep_x(0, 0)
            keep_x(1, 1)
            multiply(0)
            with dve.Fori(0, NE // 2 - 1) as i:
                for j in range(2):
                    pick(i * 2 + (j + 2), j)
                    keep_act(i * 2 + j)
                    multiply(i * 2 + (j + 1))
                    keep_x(i * 2 + (j + 2), j)
            keep_act(NE - 2)
            multiply(NE - 1)
            keep_act(NE - 1)


def stage_overflow(nc, c):
    XG, XT = view(c, MOE_AT, D), view(c, MOE_AT + 2 * D, KD, P)
    SG, AC = view(c, MOE_AT + 4 * D, FF), view(c, MOE_AT + 4 * D + FF, FF)
    ACT_T, Y = view(c, MOE_AT + 5 * D, KF, P), view(c, MOE_AT + 6 * D, D)
    idx = view(c, T_AT + 116, 1).bitcast(I32)
    gate_ps, up_ps, turn_ps, y_ps, x_ps = c.bank[0], c.bank[1], c.bank[2], c.psum_pair(2), c.psum_pair(3)
    wg, wu, wd = (c.expert_w[k][1] for k in ("gate", "up", "down"))
    idx_in, w_in, x_in, stored, step_end = (c.sem("o_idx_in"), c.sem("o_w_in"), c.sem("o_x_in"), c.sem("o_stored"),
                                            c.sem("o_step_end"))
    x_tr, x_kept, gate_mm, silu_done, up_mm = (c.sem("o_x_tr"), c.sem("o_x_kept"), c.sem("o_gate_mm"),
                                               c.sem("o_silu"), c.sem("o_up_mm"))
    act_done, act_tr, act_kept, down_mm, y_done = (c.sem("o_act"), c.sem("o_act_tr"), c.sem("o_act_kept"),
                                                   c.sem("o_down_mm"), c.sem("o_y"))

    def blocks(eng):
        return eng.value_load(c.over_i[0:1, NOVER:NOVER + 1], min_val=0, max_val=NOVER)

    with nc.Block() as block:
        @block.sync
        def _(sp):
            n = blocks(sp)
            with sp.Fori(0, NOVER) as i:
                with sp.If(i < n):
                    e = sp.value_load(c.over_i[0:1, bass.ds(i, 1)], min_val=0, max_val=NE - 1)
                    row = i * P + NE * P
                    sp.dma_start(idx, c.slot_tok[bass.ds(row, P), :]).then_inc(idx_in, 16)
                    for w, src, n_rows in ((wg, c.w_gate, D), (wu, c.w_up, D), (wd, c.w_down, FF)):
                        sp.dma_start(w, src[bass.ds(e * n_rows, n_rows), :].rearrange("(k p) n -> p k n", p=P)
                                     ).then_inc(w_in, 16)
                    sp.wait_ge(y_done, i + 1)
                    sp.dma_start(c.y_d[bass.ds(row, P), :], Y).then_inc(stored, 16)
                    sp.wait_ge(stored, i * 16 + 16)
                    sp.sem_inc(step_end, 1)

        @block.gpsimd
        def _(pool):
            n = blocks(pool)
            with pool.Fori(0, NOVER) as i:
                with pool.If(i < n):
                    pool.wait_ge(idx_in, i * 16 + 16)
                    pool.sem_inc(step_end, 1)
                    nc.gpsimd.indirect_dma_start(out=XG, out_offset=None, in_=c.h2_d,
                                                 in_offset=bass.IndirectOffsetOnAxis(ap=idx, axis=0)
                                                 ).then_inc(x_in, 16)

        @block.tensor
        def _(pe):
            mm = nc.tensor.matmul
            n = blocks(pe)
            with pe.Fori(0, NOVER) as i:
                with pe.If(i < n):
                    pe.wait_ge(x_in, i * 16 + 16)
                    for k in range(KD):
                        last = nc.tensor.transpose(x_ps[:, k * P:(k + 1) * P], XG[:, k * P:(k + 1) * P], c.ident[:])
                    last.then_inc(x_tr, 1)
                    pe.wait_ge(w_in, i * 48 + 48)
                    pe.wait_ge(x_kept, i + 1)
                    for out, w, sem in ((gate_ps, wg, gate_mm), (up_ps, wu, up_mm)):
                        for k in range(KD):
                            last = mm(out[:, :], XT[:, k, :], w[:, k, :], start=(k == 0), stop=(k == KD - 1))
                        last.then_inc(sem, 1)
                    pe.wait_ge(act_done, i + 1)
                    for k in range(KF):
                        last = nc.tensor.transpose(turn_ps[:, k * P:(k + 1) * P], AC[:, k * P:(k + 1) * P], c.ident[:])
                    last.then_inc(act_tr, 1)
                    pe.wait_ge(act_kept, i + 1)
                    for half in range(2):
                        for k in range(KF):
                            last = mm(y_ps[:, half * 512:half * 512 + 512], ACT_T[:, k, :],
                                      wd[:, k, half * 512:half * 512 + 512], start=(k == 0), stop=(k == KF - 1))
                    last.then_inc(down_mm, 1)

        @block.scalar
        def _(act):
            n = blocks(act)
            with act.Fori(0, NOVER) as i:
                with act.If(i < n):
                    act.wait_ge(gate_mm, i + 1)
                    nc.scalar.activation(SG, gate_ps[:, :], ACT.Silu).then_inc(silu_done, 1)
                    act.wait_ge(down_mm, i + 1)
                    nc.scalar.activation(Y, y_ps, ACT.Copy).then_inc(y_done, 1)

        @block.vector
        def _(dve):
            v = nc.vector
            n = blocks(dve)
            with dve.Fori(0, NOVER) as i:
                with dve.If(i < n):
                    dve.wait_ge(x_tr, i + 1)
                    v.tensor_tensor(XT, x_ps.rearrange("p (k n) -> p k n", n=P), bcast(c.g_moe[:], P),
                                    ALU.mult).then_inc(x_kept, 1)
                    dve.wait_ge(silu_done, i + 1)
                    dve.wait_ge(up_mm, i + 1)
                    v.tensor_tensor(AC, SG, up_ps[:, :], ALU.mult).then_inc(act_done, 1)
                    dve.wait_ge(act_tr, i + 1)
                    v.tensor_scalar(ACT_T.rearrange("p k n -> p (k n)"), turn_ps[:, :], 1.0, None,
                                    ALU.mult).then_inc(act_kept, 1)


def final_weights(c):
    c.wpg = [view(c, MOE_AT + 8 * D, KD, 512), view(c, MOE_GATE[0], KD, 512)]
    c.wpp = view(c, MOE_UP[0], PLE // P, D)
    c.last_rows = [view(c, T_AT + 120 + i * D, D) for i in range(3)]


def stage_final(nc, c):
    X = view(c, HT_AT, NT, D)
    YG = view(c, W_AT, 2, 2, D)
    XN = view(c, W_AT + 4 * D, 2, D)
    XT = view(c, W_AT + 6 * D, 2, KD, P)
    G = view(c, W_AT + 8 * D, 2, D)
    OUT = view(c, W_AT + 10 * D, 2, D)
    PR = view(c, Q_AT, NT, PLE)
    PT = view(c, Q_AT + NT * PLE, 2, PLE // P, P)
    junk, T = view(c, Q_AT + 3 * D, D), view(c, Q_AT + 4 * D, D)
    ST = view(c, Q_AT + 5 * D, 3, 3, NT)
    E = view(c, Q_AT + 6 * D, 2, D)
    gate_ps, e_ps, x_ps, p_ps = c.psum_pair(0), c.psum_pair(1), c.psum_pair(2), c.bank[6]
    bias_row, post_row, final_row = c.last_rows
    e_copied = c.sem("e_copied")
    p_in, pad = [c.sem("p_in"), c.sem("p_last_in")], c.sem("p_pad")
    yg_in = [c.sem(f"yg_in{j}") for j in range(2)]
    c.y_stored = [c.kept_sem(f"y_stored{j}") for j in range(2)]
    x2_part, x2_done = c.sem("x2_part"), c.sem("x2_done")
    ss, ms, rstd = ([c.sem(f"{n}_{x}") for x in ("x2", "e", "x3")] for n in ("ss", "ms", "rstd"))
    xn_done, x_tr, x_kept, p_tr, p_kept = (c.sem("xn2_done"), c.sem("x2_tr"), c.sem("x2_kept"), c.sem("p_tr"),
                                           c.sem("p_kept"))
    gate_mm, proj_mm, bias_done, sig_done, ge_done, t_done, x3_done, y_done = (
        c.sem(n) for n in ("ple_gate_mm", "ple_proj_mm", "ple_bias", "ple_sig", "ple_ge", "ple_t", "x3_done", "yf_done"))
    with nc.Block() as block:
        @block.sync
        def _(sp):
            sp.dma_start(PR[:, 0:NP, :], c.p_prompt.rearrange("(t p) d -> p t d", p=P)).then_inc(p_in[0], 16)
            sp.dma_start(PR[0:NS, NP, :], c.p_sample).then_inc(p_in[1], 16)
            for t in range(NT):
                sp.wait_ge(y_done, t + 1)
                dst = c.y_prompt[t * P:(t + 1) * P, :] if t < NP else c.y_sample
                sp.dma_start(dst, OUT[0:dst.shape[0], t % 2, :]).then_inc(c.y_stored[t % 2], 16)

        @block.gpsimd
        def _(pool):
            g = nc.gpsimd

            def gather(t):
                if t >= NT:
                    return
                if t >= 2:
                    pool.wait_ge(x2_done, t - 1)
                for r in range(2):
                    g.indirect_dma_start(out=YG[:, t % 2, r, :], out_offset=None, in_=c.y_d,
                                         in_offset=bass.IndirectOffsetOnAxis(ap=c.slot_i[:, r, t:t + 1], axis=0)
                                         ).then_inc(yg_in[t % 2], 16)

            def power(kind, t):
                pool.wait_ge(ms[kind], t + 1)
                g.tensor_tensor(ST[:, kind, 2, t:t + 1], ST[:, kind, 1, t:t + 1], c.neghalf[:, 0:1],
                                ALU.pow).then_inc(rstd[kind], 1)

            for sem in c.y_out:
                pool.wait_ge(sem, 16 * NE // 2)
            gather(0)
            gather(1)
            power(0, 0)
            gather(2)
            for t in range(NT):
                if t + 1 < NT:
                    power(0, t + 1)
                    gather(t + 3)
                power(1, t)
                power(2, t)

        @block.scalar
        def _(act):
            s = nc.scalar

            def normed(t):
                act.wait_ge(rstd[0], t + 1)
                if t >= 2:
                    act.wait_ge(x_tr, t - 1)
                s.activation(XN[:, t % 2, :], X[:, t, :], ACT.Copy, scale=ST[:, 0, 2, t:t + 1]).then_inc(xn_done, 1)

            normed(0)
            for t in range(NT):
                if t + 1 < NT:
                    normed(t + 1)
                act.wait_ge(proj_mm, t + 1)
                if t >= 2:
                    act.wait_ge(t_done, t - 1)
                s.activation(E[:, t % 2, :], e_ps, ACT.Copy).then_inc(e_copied, 1)
                act.wait_ge(bias_done, t + 1)
                s.activation(G[:, t % 2, :], G[:, t % 2, :], ACT.Sigmoid).then_inc(sig_done, 1)

        @block.tensor
        def _(pe):
            mm = nc.tensor.matmul

            def turn_p(t):
                if t == NP:
                    pe.wait_ge(p_in[1], 16)
                    pe.wait_ge(pad, 1)
                if t >= 1:
                    pe.wait_ge(p_kept, t)
                for k in range(PLE // P):
                    last = nc.tensor.transpose(p_ps[:, k * P:(k + 1) * P], PR[:, t, k * P:(k + 1) * P], c.ident[:])
                last.then_inc(p_tr, 1)

            def turn_x(t):
                pe.wait_ge(xn_done, t + 1)
                if t >= 1:
                    pe.wait_ge(x_kept, t)
                for k in range(KD):
                    last = nc.tensor.transpose(x_ps[:, k * P:(k + 1) * P], XN[:, t % 2, k * P:(k + 1) * P], c.ident[:])
                last.then_inc(x_tr, 1)

            pe.wait_ge(p_in[0], 16)
            turn_p(0)
            turn_x(0)
            pe.wait_ge(c.final_in, 16 * 6)
            for t in range(NT):
                pe.wait_ge(p_kept, t + 1)
                if t >= 1:
                    pe.wait_ge(e_copied, t)
                for half in range(2):
                    cols = slice(half * 512, half * 512 + 512)
                    for k in range(PLE // P):
                        last = mm(e_ps[:, cols], PT[:, t % 2, k, :], c.wpp[:, k, cols], start=(k == 0),
                                  stop=(k == PLE // P - 1))
                last.then_inc(proj_mm, 1)
                pe.wait_ge(x_kept, t + 1)
                if t >= 1:
                    pe.wait_ge(bias_done, t)
                for half in range(2):
                    for k in range(KD):
                        last = mm(gate_ps[:, half * 512:half * 512 + 512], XT[:, t % 2, k, :], c.wpg[half][:, k, :],
                                  start=(k == 0), stop=(k == KD - 1))
                last.then_inc(gate_mm, 1)
                if t + 1 < NT:
                    turn_p(t + 1)
                    turn_x(t + 1)

        @block.vector
        def _(dve):
            v = nc.vector
            v.memset(PR[NS:P, NP, :], 0.0).then_inc(pad, 1)

            def mean_square(kind, t, src):
                v.tensor_tensor_reduce(junk, src, src, 1.0, 0.0, ALU.mult, ALU.add,
                                       ST[:, kind, 0, t:t + 1]).then_inc(ss[kind], 1)
                dve.wait_ge(ss[kind], t + 1)
                v.tensor_scalar(ST[:, kind, 1, t:t + 1], ST[:, kind, 0, t:t + 1], 1.0 / D, EPS, ALU.mult,
                                ALU.add).then_inc(ms[kind], 1)

            def x2(t):
                dve.wait_ge(yg_in[t % 2], 32 * (t // 2 + 1))
                v.scalar_tensor_tensor(out=X[:, t, :], in0=YG[:, t % 2, 0, :], scalar=c.w_tok[:, 0, t:t + 1],
                                       in1=X[:, t, :], op0=ALU.mult, op1=ALU.add).then_inc(x2_part, 1)
                dve.wait_ge(x2_part, t + 1)
                v.scalar_tensor_tensor(out=X[:, t, :], in0=YG[:, t % 2, 1, :], scalar=c.w_tok[:, 1, t:t + 1],
                                       in1=X[:, t, :], op0=ALU.mult, op1=ALU.add).then_inc(x2_done, 1)
                dve.wait_ge(x2_done, t + 1)
                mean_square(0, t, X[:, t, :])

            def keep_p(t):
                dve.wait_ge(p_tr, t + 1)
                if t >= 2:
                    dve.wait_ge(proj_mm, t - 1)
                v.tensor_copy(PT[:, t % 2], p_ps[:, 0:PLE].rearrange("p (k n) -> p k n", n=P)).then_inc(p_kept, 1)

            def keep_x(t):
                dve.wait_ge(x_tr, t + 1)
                if t >= 2:
                    dve.wait_ge(gate_mm, t - 1)
                v.tensor_tensor(XT[:, t % 2], x_ps.rearrange("p (k n) -> p k n", n=P), bcast(c.g_ple[:], P),
                                ALU.mult).then_inc(x_kept, 1)

            def biased(t):
                dve.wait_ge(gate_mm, t + 1)
                if t >= 2:
                    dve.wait_ge(t_done, t - 1)
                v.tensor_tensor(G[:, t % 2, :], gate_ps, bias_row, ALU.add).then_inc(bias_done, 1)

            def e_square(t):
                dve.wait_ge(e_copied, t + 1)
                mean_square(1, t, E[:, t % 2, :])

            def x3(t):
                dve.wait_ge(sig_done, t + 1)
                v.tensor_tensor(G[:, t % 2, :], G[:, t % 2, :], post_row, ALU.mult).then_inc(ge_done, 1)
                dve.wait_ge(ge_done, t + 1)
                dve.wait_ge(rstd[1], t + 1)
                if t:
                    dve.wait_ge(x3_done, t)
                v.scalar_tensor_tensor(out=T, in0=E[:, t % 2, :], scalar=ST[:, 1, 2, t:t + 1], in1=G[:, t % 2, :], op0=ALU.mult,
                                       op1=ALU.mult).then_inc(t_done, 1)
                dve.wait_ge(t_done, t + 1)
                dve.wait_ge(xn_done, t + 1)
                v.tensor_tensor(X[:, t, :], X[:, t, :], T, ALU.add).then_inc(x3_done, 1)
                dve.wait_ge(x3_done, t + 1)
                mean_square(2, t, X[:, t, :])

            def y(t):
                dve.wait_ge(rstd[2], t + 1)
                if t >= 2:
                    dve.wait_ge(c.y_stored[t % 2], 16 * (t // 2))
                v.scalar_tensor_tensor(out=OUT[:, t % 2, :], in0=X[:, t, :], scalar=ST[:, 2, 2, t:t + 1],
                                       in1=final_row, op0=ALU.mult, op1=ALU.mult).then_inc(y_done, 1)

            x2(0)
            keep_p(0)
            keep_x(0)
            dve.wait_ge(c.final_in, 16 * 6)
            for t in range(NT):
                if t + 1 < NT:
                    x2(t + 1)
                if t:
                    y(t - 1)
                e_square(t)
                biased(t)
                if t + 1 < NT:
                    keep_p(t + 1)
                    keep_x(t + 1)
                x3(t)
            y(NT - 1)


def program(nc, c):
    with ExitStack() as ctx:
        start(nc, c, ctx)
        stage_norm(nc, c)
        stage_project(nc, c)
        stage_mlp(nc, c)
        stage_prompt_attention(nc, c)
        stage_sample_attention(nc, c)
        release(nc, c)
        stage_merge(nc, c)
        stage_out(nc, c)
        stage_route(nc, c)
        release(nc, c)
        stage_moe(nc, c)
        stage_overflow(nc, c)
        stage_final(nc, c)
        finish(nc, c)


def finish(nc, c):
    with nc.Block() as block:
        @block.sync
        def _(sp):
            for j in range(2):
                sp.wait_ge(c.y_stored[j], 16 * ((NT + 1 - j) // 2))
            sp.wait_ge(c.out_rows, 16 * 7)
            sp.wait_ge(c.sufd_out, 16 * H)
            sp.wait_ge(c.consts_in, 16 * 6)
            for sem in c.w_in_sem + [c.w_vb_in, c.blank_out, c.table_out]:
                sp.wait_ge(sem, 16)
            for sem in c.h2_out:
                sp.wait_ge(sem, 16 * 3)
            for sem in c.y_out + c.expert_in["gate"] + c.expert_in["up"] + c.expert_in["down"]:
                sp.wait_ge(sem, 16 * NE // 2)
            sp.wait_ge(c.final_in, 16 * 6)


INPUTS = ["x_prompt", "x_sample", "p_prompt", "p_sample", "cache_k", "cache_v", "cache_logf", "page_table",
          "norm_mix_g", "w_in", "b_f", "ln_v_g", "ln_v_b", "w_spatial", "b_spatial", "w_up_a", "w_up_b", "w_o",
          "norm_moe_g", "w_router_group", "b_router_group", "w_router_expert", "b_router_expert", "w_exp_gate",
          "w_exp_up", "w_exp_down", "norm_ple_g", "w_ple_gate", "b_ple_gate", "w_ple_proj", "norm_ple_post_g",
          "norm_final_g"]
OUTPUTS = [("y_prompt", (1, SEQ, D)), ("y_sample", (DB, DT, D)), ("new_k_p", (1, 1, SEQ, H, DH)),
           ("new_v_p", (1, 1, SEQ, H, DH)), ("new_lf_p", (1, 1, SEQ, H)), ("new_k_s", (1, DB, DT, H, DH)),
           ("new_v_s", (1, DB, DT, H, DH)), ("new_lf_s", (1, DB, DT, H)), ("new_cv_s", (1, DB, DT, WA))]


def views(c, a):
    def by_partition(w, n=1):
        return w.rearrange("(k p) n -> p k n", p=P)

    def row(w):
        return w.partition_broadcast(P)

    c.x_prompt = a["x_prompt"][0]
    c.x_sample = a["x_sample"].rearrange("b t d -> (b t) d")
    c.p_prompt = a["p_prompt"][0, 0]
    c.p_sample = a["p_sample"][0].rearrange("b t d -> (b t) d")
    c.cache_k = a["cache_k"][0].rearrange("n s h d -> (n s) (h d)")
    c.cache_v = a["cache_v"][0].rearrange("n s h d -> (n s) (h d)")
    c.cache_logf = a["cache_logf"][0].rearrange("n s h -> n (s h)")
    c.page_rows = a["page_table"].rearrange("b (g o) -> (b g) o", o=1)
    c.page_table = a["page_table"]
    c.n_pool = a["cache_k"].shape[1]
    c.w_in = by_partition(a["w_in"][0])
    c.norm_mix_g, c.norm_moe_g, c.norm_ple_g = (a[g][0].rearrange("(k p) -> p k", p=P)
                                                for g in ("norm_mix_g", "norm_moe_g", "norm_ple_g"))
    c.b_f, c.ln_v_g, c.ln_v_b = row(a["b_f"][0]), row(a["ln_v_g"][0]), row(a["ln_v_b"][0])
    c.b_router_group, c.b_router_expert = row(a["b_router_group"][0]), row(a["b_router_expert"][0])
    c.b_ple_gate, c.norm_ple_post_g = row(a["b_ple_gate"][0]), row(a["norm_ple_post_g"][0])
    c.norm_final_g = row(a["norm_final_g"])
    c.w_spatial, c.b_spatial = a["w_spatial"][0], a["b_spatial"][0]
    c.w_up_a, c.w_up_b = by_partition(a["w_up_a"][0]), by_partition(a["w_up_b"][0])
    c.w_o = by_partition(a["w_o"][0])
    c.w_router_group, c.w_router_expert = by_partition(a["w_router_group"][0]), by_partition(a["w_router_expert"][0])
    c.w_gate = a["w_exp_gate"][0].rearrange("e d f -> (e d) f")
    c.w_up = a["w_exp_up"][0].rearrange("e d f -> (e d) f")
    c.w_down = a["w_exp_down"][0].rearrange("e f d -> (e f) d")
    c.w_ple_gate, c.w_ple_proj = by_partition(a["w_ple_gate"][0]), by_partition(a["w_ple_proj"][0])


def kernel(**inputs):
    import concourse.bacc as bacc
    from concourse.bass_utils import run_bass_kernel_spmd as run

    nc = bacc.Bacc("TRN2", target_bir_lowering=False, num_devices=1)
    arrays, a, c = {}, {}, Core()
    for name in INPUTS:
        x = np.ascontiguousarray(inputs[name])
        arrays["in_" + name] = x
        a[name] = nc.dram_tensor("in_" + name, x.shape, mybir.dt.from_np(x.dtype), kind="ExternalInput").ap()
    views(c, a)
    out = {}
    for name, shape in OUTPUTS:
        o = nc.dram_tensor("out_" + name, shape, F32, kind="ExternalOutput").ap()
        if len(shape) == 5:
            o = o.rearrange("l b t h d -> (l b t) (h d)")
        elif len(shape) == 4:
            o = o.rearrange("l b t h -> (l b t) h")
        else:
            o = o.rearrange("b t d -> (b t) d")
        out[name] = o
    c.y_prompt, c.y_sample = out["y_prompt"], out["y_sample"]
    c.new_k_p, c.new_v_p, c.new_lf_p = out["new_k_p"], out["new_v_p"], out["new_lf_p"]
    c.new_k_s, c.new_v_s, c.new_lf_s, c.new_cv_s = out["new_k_s"], out["new_v_s"], out["new_lf_s"], out["new_cv_s"]
    c.sufd = nc.dram_tensor("suffix_bias", (H, DB, PAST), F32).ap()
    c.cum_d = nc.dram_tensor("cum_forget", (H, SEQ + NS), F32).ap()
    c.h2_d = nc.dram_tensor("moe_in", (TOK, D), F32).ap()
    c.slot_tok = nc.dram_tensor("slot_token", (SLOTS, 1), I32).ap()
    c.y_d = nc.dram_tensor("moe_out", (SLOTS, D), F32).ap()
    program(nc, c)
    r = run(nc, [arrays], core_ids=[0]).results[0]
    return tuple(r["out_" + name] for name, _ in OUTPUTS)
```
